# Optimizing a Trainium2 kernel written in Bass

```python
import math
import jax, jax.numpy as jnp
from jax import lax
import numpy as np

D_MODEL = 1024
BATCH = 1
SEQ = 1024
DEPTH = 2
DEC_BATCH = 8
DEC_SEQ = 4
PAST_LEN = 8192
PAGE_SIZE = 128

N_MIXERS = 2
BRANCH = D_MODEL
HEAD_DIM = 128
N_HEADS = BRANCH // HEAD_DIM
HEAD_DK = HEAD_DIM
HEAD_DV = HEAD_DIM
CONV_W = 3
HGRN_CHUNK = 64
N_CONV_LAYERS = (DEPTH + 1) // 2
N_HGRN_LAYERS = DEPTH // 2
RMS_EPS = 1e-6
LOG_F_FLOOR = -20.0

kernel_name = "hybrid_shortconv_hgrn2_decode_step"

def rms_norm(x, g):
    xf = x.astype(jnp.float32)
    y = xf * lax.rsqrt(jnp.mean(xf * xf, axis=-1, keepdims=True) + RMS_EPS)
    return (y * g.astype(jnp.float32)).astype(x.dtype)

def conv_branch(h, w_in, w_conv, w_out, buf):
    T = h.shape[1]
    proj = h @ w_in
    v, bg, cg, z = jnp.split(proj, 4, axis=-1)
    u = cg * v
    u_ext = jnp.concatenate([buf.astype(u.dtype), u], axis=1)
    conv = w_conv[0] * u_ext[:, 0:T]
    for j in range(1, CONV_W):
        conv = conv + w_conv[j] * u_ext[:, j:j + T]
    new_buf = u_ext[:, -(CONV_W - 1):]
    y = (bg * conv * jax.nn.silu(z)) @ w_out
    return y, new_buf

def hgrn2_chunked(q, k, v, log_f, s0):
    b, T = q.shape[:2]
    C = math.gcd(T, HGRN_CHUNK)
    nc = T // C

    def to_chunks(a):
        return a.reshape(b, nc, C, a.shape[2], a.shape[3]).transpose(1, 0, 3, 2, 4)

    mask = jnp.tril(jnp.ones((C, C), dtype=bool))[None, None, :, :, None]

    def step(S, inp):
        qc, kc, vc, gc = inp
        bcum = jnp.cumsum(gc, axis=2)
        rel = jnp.where(mask, bcum[:, :, :, None, :] - bcum[:, :, None, :, :], -jnp.inf)
        A = jnp.einsum('bhtk,bhtsk,bhsk->bhts', qc, jnp.exp(rel), kc)
        o = jnp.einsum('bhts,bhsv->bhtv', A, vc) + jnp.einsum('bhtk,bhkv->bhtv', qc * jnp.exp(bcum), S)
        b_last = bcum[:, :, -1:, :]
        S = jnp.exp(b_last[:, :, 0, :])[..., None] * S + jnp.einsum(
            'bhsk,bhsv->bhkv', kc * jnp.exp(b_last - bcum), vc)
        return S, o

    S, o = lax.scan(step, s0, (to_chunks(q), to_chunks(k), to_chunks(v), to_chunks(log_f)))
    o = o.transpose(1, 0, 3, 2, 4).reshape(b, T, q.shape[2], v.shape[-1])
    return o, S

def hgrn_branch(h, w_in, lb, g_onorm, w_out, s0):
    b, T = h.shape[:2]
    proj = h @ w_in
    q, fpre, inp, z = jnp.split(proj, 4, axis=-1)
    shp = (b, T, N_HEADS, HEAD_DK)
    q = jax.nn.silu(q.astype(jnp.float32)).reshape(shp) * (HEAD_DK ** -0.5)
    fpre = fpre.astype(jnp.float32).reshape(shp)
    vv = inp.astype(jnp.float32).reshape(b, T, N_HEADS, HEAD_DV)
    lb = lb.reshape(N_HEADS, HEAD_DK)
    log_f = jnp.logaddexp(jnp.log(lb), jnp.log1p(-lb) + jax.nn.log_sigmoid(fpre))
    log_f = jnp.maximum(log_f, LOG_F_FLOOR)
    k = -jnp.expm1(log_f)
    o, S = hgrn2_chunked(q, k, vv, log_f, s0)
    o = rms_norm(o, g_onorm).reshape(b, T, BRANCH).astype(h.dtype)
    y = (o * jax.nn.silu(z)) @ w_out
    return y, S

def setup_inputs(seed: int = 0) -> dict:
    key = jax.random.key(seed)
    ks = jax.random.split(key, 11)
    E = BRANCH
    return {
        "x_prompt": jax.random.normal(ks[0], (BATCH, SEQ, D_MODEL), jnp.float32),
        "x_sample": jax.random.normal(ks[1], (DEC_BATCH, DEC_SEQ, D_MODEL), jnp.float32),
        "state_conv": jax.random.normal(ks[2], (N_CONV_LAYERS, DEC_BATCH, CONV_W - 1, E), jnp.float32),
        "state_hgrn": 0.5 * jax.random.normal(ks[3], (N_HGRN_LAYERS, DEC_BATCH, N_HEADS, HEAD_DK, HEAD_DV), jnp.float32),
        "norm_pre": 1.0 + 0.05 * jax.random.normal(ks[4], (DEPTH, D_MODEL), jnp.float32),
        "w_in": jax.random.normal(ks[5], (DEPTH, D_MODEL, 4 * E), jnp.float32) * D_MODEL ** -0.5,
        "conv_w": jax.random.normal(ks[6], (N_CONV_LAYERS, CONV_W, E), jnp.float32) * CONV_W ** -0.5,
        "hgrn_lb_logits": 0.5 * jax.random.normal(ks[7], (N_HGRN_LAYERS, E), jnp.float32),
        "hgrn_onorm": 1.0 + 0.05 * jax.random.normal(ks[8], (N_HGRN_LAYERS, HEAD_DV), jnp.float32),
        "w_out": jax.random.normal(ks[9], (DEPTH, E, D_MODEL), jnp.float32) * E ** -0.5,
        "norm_post": 1.0 + 0.05 * jax.random.normal(ks[10], (DEPTH, D_MODEL), jnp.float32),
    }

def reference(x_prompt, x_sample, state_conv, state_hgrn, norm_pre, w_in, conv_w,
              hgrn_lb_logits, hgrn_onorm, w_out, norm_post):
    lb_all = jnp.cumsum(jax.nn.softmax(hgrn_lb_logits.astype(jnp.float32), axis=0), axis=0)
    lb_all = lb_all - lb_all[0:1]

    xp, xs = x_prompt, x_sample
    conv_p, conv_s, hgrn_p, hgrn_s = [], [], [], []
    for i in range(DEPTH):
        j = i // N_MIXERS
        hp = rms_norm(xp, norm_pre[i])
        hs = rms_norm(xs, norm_pre[i])
        if i % N_MIXERS == 0:
            buf0 = jnp.zeros((xp.shape[0], CONV_W - 1, BRANCH), xp.dtype)
            yp, bp = conv_branch(hp, w_in[i], conv_w[j], w_out[i], buf0)
            ys, bs = conv_branch(hs, w_in[i], conv_w[j], w_out[i], state_conv[j])
            conv_p.append(bp.astype(xp.dtype))
            conv_s.append(bs.astype(state_conv.dtype))
        else:
            s0 = jnp.zeros((xp.shape[0], N_HEADS, HEAD_DK, HEAD_DV), jnp.float32)
            yp, Sp = hgrn_branch(hp, w_in[i], lb_all[j], hgrn_onorm[j], w_out[i], s0)
            ys, Ss = hgrn_branch(hs, w_in[i], lb_all[j], hgrn_onorm[j], w_out[i],
                                 state_hgrn[j].astype(jnp.float32))
            hgrn_p.append(Sp.astype(xp.dtype))
            hgrn_s.append(Ss.astype(state_hgrn.dtype))
        xp = xp + rms_norm(yp, norm_post[i])
        xs = xs + rms_norm(ys, norm_post[i])

    return (xp, xs, jnp.stack(conv_p), jnp.stack(conv_s), jnp.stack(hgrn_p), jnp.stack(hgrn_s))


_drawn_inputs = setup_inputs


def setup_inputs(seed=0):
    import zlib

    import numpy as np

    out = dict(_drawn_inputs(seed))
    spreads = {}
    factors = {}
    for name, (base, spread) in spreads.items():
        noise = np.random.default_rng([zlib.crc32(name.encode()), seed]).standard_normal(out[name].shape)
        drawn = base * np.exp(spread * noise) if base else spread * noise
        out[name] = __import__('jax').numpy.asarray(drawn.astype(out[name].dtype))
    for name, factor in factors.items():
        out[name] = (out[name] * factor).astype(out[name].dtype)
    return out
```

```python
from contextlib import ExitStack

import concourse.bass as bass
from concourse import mybir

F32 = mybir.dt.float32
F32R = mybir.dt.float32r
U8 = mybir.dt.uint8
ALU = mybir.AluOpType
ACT = mybir.ActivationFunctionType
AX = mybir.AxisListType

P = 128
D = 1024
KT = D // P
NP = 1024
NB, NS = 8, 4
NSAMP = NB * NS
T = NP + NSAMP
CH = T // 3
NCH = 3
CK = NP // P
EPS = 1e-6
F_FLOOR = 2.061153622438558e-09
QSCALE = float(P) ** -0.5
LEVELS = (1, 2, 4, 8, 16, 32, 64)
SUBS = ((0, 128), (128, 128), (256, 96))


class Events:

    def __init__(self, sem, names):
        self.sem, self.names = sem, list(names)
        self.index = {n: k for k, n in enumerate(self.names)}
        self.cursor = 0

    def now(self, name):
        assert self.names[self.cursor % len(self.names)] == name, (name, self.names[self.cursor % len(self.names)])
        self.cursor += 1
        return self.sem

    def at(self, round_, name):
        return round_ * len(self.names) + self.index[name] + 1


def build(nc, x_prompt, x_sample, state_conv, state_hgrn, norm_pre, w_in, conv_w, lb_logits, onorm,
          w_out, norm_post, y_prompt, y_sample, conv_p, conv_s, hgrn_p, hgrn_s):
    ctx = ExitStack()
    with ctx:
        def sb(name, shape, dt=F32):
            return ctx.enter_context(nc.sbuf_tensor(name, shape, dt))

        def sem(name):
            return ctx.enter_context(nc.semaphore(name))

        REG = 2 * KT * T
        reg_a = sb("reg_a", [P, REG], F32R)
        reg_b = sb("reg_b", [P, REG], F32R)
        wsplit = sb("wsplit", [P, 2, 2, KT, P], F32R)
        wraw = sb("wraw", [P, 2, KT, P])

        def halves(reg):
            return [reg[:, i * KT * T:(i + 1) * KT * T].rearrange("p (k t) -> p k t", k=KT) for i in range(2)]

        def wout_tile(reg, m):
            if m < 2:
                return [wsplit[:, m, i] for i in range(2)]
            at = 2 * (m - 2) * KT * P
            return [reg[:, at + i * KT * P:at + (i + 1) * KT * P].rearrange("p (k c) -> p k c", k=KT)
                    for i in range(2)]

        ident = sb("ident", [P, P])
        cst = sb("cst", [P, 65])
        PRE, POST, CW, LBL, ONRM = 0, 2 * KT, 4 * KT, 7 * KT, 8 * KT
        lb = sb("lb", [P, 2, KT])
        eps = sb("eps", [P, 1])
        masks = {m: sb(f"mask{m}", [P, P // 2], U8) for m in LEVELS if m < 64}
        bmask = sb("bmask", [P, NB])
        small = sb("small", [P, 48])

        ARENA = 11744
        arena = sb("arena", [P, ARENA])

        class Plan:
            def __init__(self, at=0):
                self.at = at

            def take(self, n):
                self.at += n
                assert self.at <= ARENA, self.at
                return arena[:, self.at - n:self.at]

        pl = Plan()
        st_x = [pl.take(D) for _ in range(3)]
        st_n = [pl.take(D) for _ in range(2)]
        st_t = [pl.take(D) for _ in range(2)]
        st_row = pl.take(D)
        st_vec = pl.take(P)
        st_scr = pl.take(D)
        st_lb = pl.take(4 * KT).rearrange("p (a k) -> p a k", a=4)
        c_st = pl.take(KT * 2 * NB)
        c_last = pl.take(KT * 18)
        st_ms = pl.take(6 * 64)
        c_last18 = st_row
        pl = Plan()
        UL = 2 + NP
        c_v = pl.take(T)
        c_u = pl.take(UL + NB * (NS + 2))
        c_acc = pl.take(T)
        c_g = pl.take(T)
        c_o = pl.take(T)
        c_w = pl.take(3)
        pl = Plan()
        r_am = pl.take(CK * P)
        r_kt = pl.take((CK + 1) * P)
        r_K = pl.take(T)
        r_Q, r_f, r_q, r_kr, r_vr, r_g = [pl.take(T) for _ in range(6)]
        r_vt = pl.take((CK + 1) * P)
        r_s = pl.take(CK * P)
        assert pl.at <= ARENA
        r_tt = sb("r_tt", [P, T // 2])
        r_qb = sb("r_qb", [P, NB * (NSAMP + NS)])
        r_os = sb("r_os", [P, P])
        r_as = sb("r_as", [NSAMP, NSAMP])
        lbh = sb("lbh", [P, 2])
        r_o = r_kr
        r_sq = r_Q
        pl = Plan()
        o_y = [pl.take(KT * CH).rearrange("p (m t) -> p m t", m=KT) for _ in range(2)]
        o_sq = [pl.take(CH) for _ in range(2)]
        o_acc = pl.take(CH)
        o_rb = pl.take(CH)
        o_t = [pl.take(CH) for _ in range(2)]
        pl2 = Plan(pl.at)
        o_t2, o_acc2 = pl.take(CH), pl.take(CH)
        o_x = pl.take(3 * D)
        o_x1 = pl2.take(KT * CH).rearrange("p (m t) -> p m t", m=KT)
        o_yt = pl2.take(D)
        ones = sb("ones", [P, P])

        bank = [ctx.enter_context(nc.psum_tensor(f"bank{i}", [P, 512], F32)) for i in range(8)]
        xT_dram = nc.dram_tensor("x1_scratch", (P, KT, T), F32, kind="Internal").ap()

        x_in = [sem(f"x_in{i}") for i in range(3)]
        vec_in, cst_in = sem("vec_in"), sem("cst_in")
        w_in_s = [sem(f"w_loaded{i}") for i in range(2)]
        w_hi, w_lo = sem("w_hi"), sem("w_lo")
        proj_done = sem("proj_done")
        bank_free = [sem(f"bank_free{i}") for i in range(3)]
        pool_ev = Events(sem("pool_ev"), ["id0", "id", "ones"] + [f"m{m}{s}" for m in LEVELS if m < 64 for s in "abc"]
                         + ["b0", "b1", "b2", "qb0"])
        S_AN = Events(sem("start_act_norm"), ["sq", "sd"])
        S_AT = Events(sem("start_act_split"), ["hi"])
        S_DN = Events(sem("start_dve_norm"), ["rs", "xn"])
        S_DT = Events(sem("start_dve_split"), ["ta", "tb", "lo"])
        S_PE = Events(sem("start_pe"), ["ta", "tb"])
        K_PE, K_DVE, K_ACT = sem("const_pe"), sem("const_dve"), sem("const_act")
        C_ACT = Events(sem("conv_act"), ["g0", "g1", "g2", "h0", "h1", "h2"])
        C_DVE = Events(sem("conv_dve"), ["st", "cw", "a0", "a1", "a2", "last", "o0", "o1", "o2", "l0", "l1", "l2"])
        tail_pe, tail_act = sem("state_pe"), sem("state_act")
        A_SQ = Events(sem("out_act_sq"), [f"sq{m}" for m in range(KT)])
        V_ACC = Events(sem("out_dve_acc"), [f"a{m}" for m in range(KT)])
        A_PO = Events(sem("out_act_post"), ["sd1"] + [f"s{m}" for m in range(KT)] + ["sd2"] + [f"h{m}" for m in range(KT)])
        V_PO = Events(sem("out_dve_post"), ["rb1"] + sum([[f"t{m}", f"x{m}"] + [f"a{m - 1}"] * (m > 0) for m in range(KT)], [])
                      + [f"a{KT - 1}", "rb2"] + sum([[f"u{m}"] + [f"l{m - 1}"] * (m > 0) for m in range(KT)], [])
                      + [f"l{KT - 1}"])
        P_PO = Events(sem("out_pe_post"), ["ss1"] + [f"xt{m}" for m in range(KT)] + ["ss2"])
        A_P2 = Events(sem("out2_act_post"), ["sd1", "y0", "y1", "y2"])
        V_P2 = Events(sem("out2_dve_post"), ["rb1", "t0"] + sum([[f"t{m}"] * (m < KT) + [f"x{m - 1}"] for m in range(1, KT + 1)], []))
        P_P2 = Events(sem("out2_pe_post"), ["ss1", "y0", "y1", "y2"])
        q_sig, z_sig = sem("q_sig"), sem("z_sig")
        PR = Events(sem("rec_pe"), ["dg", "vt", "L1", "L2", "L4", "kst", "L8", "os", "L16", "us", "L32", "L64",
                                    "kt", "u", "o0", "o1"])
        VR = Events(sem("rec_dve"), ["lb", "k", "fa", "f", "q1", "am", "as", "vs", "w1", "c1", "u1", "w2", "c2",
                                     "u2", "qb", "w4", "c4", "u4", "w8", "c8", "u8", "w16", "c16", "u16", "ss",
                                     "sn0", "snew", "w32", "c32", "u32", "w64", "c64", "u64"]
                    + [f"s{c}" for c in range(CK)] + ["r0", "r1", "rs", "rss", "on0", "on1", "ons"])
        AR = Events(sem("rec_act"), ["vt", "kts", "os", "sqs", "kt", "sq0", "sq1", "sd", "sds"])
        pool_rec = sem("rec_pool")
        ot_done, o_rdy, o_hi, o_lo = sem("ot_done"), sem("o_rdy"), sem("o_hi"), sem("o_lo")
        s0_in, s0_out, sp_out = sem("s0_in"), sem("s0_out"), sem("sp_out")
        xr_in = sem("xr_in")
        spill = [sem(f"spill{c}") for c in range(NCH)]
        yout, cout = sem("y_out"), sem("conv_out")

        NW1, NW2, NW3 = 4 * KT, 5 * KT, 9 * KT
        G_OUT1, G_IN2, G_OUT2 = 3 * NW1, 3 * NW1 + 3 * KT, 6 * NW1 + 3 * KT

        def wsrc(w, col):
            return w[:, bass.ds(col, P)].rearrange("(k p) c -> p k c", p=P)

        def emptied(n):
            return n + 1

        def out_use(base, m):
            return base + 2 * KT + m + 1

        block = ctx.enter_context(nc.Block())

        def store_y(sp, c):
            for s, (o, r) in enumerate(SUBS):
                tok = c * CH + o
                n = min(r, NP - tok)
                sp.wait_ge(A_P2.sem, A_P2.at(c, f"y{s}"))
                sp.dma_start(y_prompt[0, tok:tok + n, :], o_yt[0:n, :]).then_inc(yout, 16)
                if n < r:
                    sp.dma_start(y_sample.rearrange("b s d -> (b s) d"), o_yt[n:r, :]).then_inc(yout, 16)

        @block.sync
        def _(sp):
            def load_w(n, src, slot, half, guard=True):
                if guard:
                    sp.wait_ge(w_lo, n - 1)
                sp.dma_start(wraw[:, slot], src).then_inc(w_in_s[slot], 16)

            for src, row, n in ((norm_pre, PRE, 2), (norm_post, POST, 2), (conv_w[0], CW, 3), (lb_logits, LBL, 1)):
                sp.dma_start(st_vec[row:row + n * KT, :], src.rearrange("l (k p) -> (l k) p", p=P)).then_inc(vec_in, 16)
            sp.dma_start(st_vec[ONRM:ONRM + 1, :], onorm).then_inc(vec_in, 16)
            sp.dma_start(st_row[0:2 * NB, :], state_conv[0].rearrange("b w c -> (b w) c")).then_inc(cst_in, 16)
            for i in range(9):
                r = P if i < 8 else NSAMP
                if i >= 3:
                    sp.wait_ge(S_DN.sem, S_DN.at(i - 3, "xn"))
                src = x_prompt[0, i * P:(i + 1) * P, :] if i < 8 else x_sample.rearrange("b s d -> (b s) d")
                sp.dma_start(st_x[i % 3][0:r, :], src).then_inc(x_in[i % 3], 16)
                if i == 2:
                    load_w(0, wsrc(w_in[0], 0), 0, 0, False)
                    load_w(1, wsrc(w_in[0], 2 * D), 1, 0, False)
            COL0 = (0, 2 * D, D, 3 * D)
            for t in (2, 3):
                load_w(t, wsrc(w_in[0], COL0[t]), t % 2, 1)
            with sp.Fori(1, KT) as j:
                for t in range(4):
                    load_w(j * 4 + t, wsrc(w_in[0], j * P + COL0[t]), t % 2, None)
            def load_xrows(c):
                if c >= 1:
                    sp.wait_ge(P_PO.sem, P_PO.at(c - 1, f"xt{KT - 1}"))
                else:
                    sp.wait_ge(C_DVE.sem, C_DVE.at(KT - 1, "l2"))
                    sp.wait_ge(tail_pe, 2)
                for s, (o, r) in enumerate(SUBS):
                    tok = c * CH + o
                    n = min(r, NP - tok)
                    sp.dma_start(o_x[0:n, s * D:(s + 1) * D], x_prompt[0, tok:tok + n, :]).then_inc(xr_in, 16)
                    if n < r:
                        sp.dma_start(o_x[n:r, s * D:(s + 1) * D], x_sample.rearrange("b s d -> (b s) d")).then_inc(xr_in, 16)

            for m in range(KT):
                load_w(NW1 + m, wsrc(w_out[0], m * P), m % 2, None)
            load_xrows(0)
            sp.wait_ge(tail_act, 2)
            sp.dma_start(conv_p[0, 0], c_last18[0:2, :]).then_inc(cout, 16)
            sp.dma_start(conv_s[0].rearrange("b w c -> (b w) c"), c_last18[2:18, :]).then_inc(cout, 16)

            def spill_x1(c):
                sp.wait_ge(V_PO.sem, V_PO.at(c, f"x{KT - 1}"))
                sp.dma_start(xT_dram[:, :, c * CH:(c + 1) * CH], o_y[c % 2]).then_inc(spill[c], 16)

            QC, FC, VC, ZC = 0, D, 2 * D, 3 * D
            load_w(NW2, wsrc(w_in[1], QC), 0, None)
            load_w(NW2 + 1, wsrc(w_in[1], VC), 1, None)
            load_xrows(1)
            spill_x1(0)
            load_xrows(2)
            spill_x1(1)
            load_w(NW2 + 2, wsrc(w_in[1], FC), 0, None)
            spill_x1(2)
            with sp.Fori(1, KT) as j:
                for t, col in enumerate((QC, ZC - P, VC, FC)):
                    load_w(NW2 - 1 + t + j * 4, wsrc(w_in[1], j * P + col), (1 + t) % 2, None)
            load_w(NW3 - 1, wsrc(w_in[1], ZC + (KT - 1) * P), 1, None)
            for m in range(KT):
                load_w(NW3 + m, wsrc(w_out[1], m * P), m % 2, None)
            for c in range(NCH):
                sp.wait_ge(spill[c], 16)
            sp.wait_ge(s0_out, KT * 16)
            sp.wait_ge(sp_out, KT * 16)
            sp.wait_ge(o_lo, KT)
            for c in range(NCH):
                if c >= 1:
                    sp.wait_ge(V_P2.sem, V_P2.at(c - 1, f"x{KT - 1}"))
                sp.dma_start(o_x1, xT_dram[:, :, c * CH:(c + 1) * CH]).then_inc(xr_in, 16)
                if c >= 1:
                    store_y(sp, c - 1)
            store_y(sp, NCH - 1)
            sp.wait_ge(cout, 32)
            sp.wait_ge(yout, 16 * (3 * NCH + 1))

        @block.gpsimd
        def _(pool):
            pool.memset(ident[:, :], 0.0).then_inc(pool_ev.now("id0"), 1)
            pool.wait_ge(pool_ev.sem, pool_ev.at(0, "id0"))
            pool.affine_select(out=ident[:, :], in_=ident[:, :], compare_op=ALU.not_equal, fill=1.0, base=0,
                               pattern=[[-1, P]], channel_multiplier=1).then_inc(pool_ev.now("id"), 1)
            pool.memset(ones[:, :], 1.0).then_inc(pool_ev.now("ones"), 1)
            for i, m in enumerate(LEVELS[:-1]):
                scr = st_ms[:, 64 * i:64 * i + 64]
                v = scr.rearrange("p (b r) -> p b r", r=m)
                nb = 64 // m
                pool.memset(scr, 1.0).then_inc(pool_ev.now(f"m{m}a"), 1)
                pool.wait_ge(pool_ev.sem, pool_ev.at(0, f"m{m}a"))
                pool.affine_select(out=v, in_=v, compare_op=ALU.is_ge, fill=0.0, base=0,
                                   pattern=[[-2 * m, nb], [0, m]], channel_multiplier=1).then_inc(pool_ev.now(f"m{m}b"), 1)
                pool.wait_ge(pool_ev.sem, pool_ev.at(0, f"m{m}b"))
                pool.affine_select(out=v, in_=v, compare_op=ALU.is_ge, fill=0.0, base=m - 1,
                                   pattern=[[2 * m, nb], [0, m]], channel_multiplier=-1).then_inc(pool_ev.now(f"m{m}c"), 1)
            pool.memset(bmask[:, :], 1.0).then_inc(pool_ev.now("b0"), 1)
            pool.wait_ge(pool_ev.sem, pool_ev.at(0, "b0"))
            pool.affine_select(out=bmask[:, :], in_=bmask[:, :], compare_op=ALU.is_ge, fill=0.0, base=0,
                               pattern=[[-NS, NB]], channel_multiplier=1).then_inc(pool_ev.now("b1"), 1)
            pool.wait_ge(pool_ev.sem, pool_ev.at(0, "b1"))
            pool.affine_select(out=bmask[:, :], in_=bmask[:, :], compare_op=ALU.is_ge, fill=0.0, base=NS - 1,
                               pattern=[[NS, NB]], channel_multiplier=-1).then_inc(pool_ev.now("b2"), 1)
            pool.memset(r_qb[:, :], 0.0).then_inc(pool_ev.now("qb0"), 1)

            def spread_v(h):
                pool.wait_ge(VR.sem, VR.at(h, "vs"))
                pool.tensor_tensor(r_kt[0:NSAMP, 0:NB * P].rearrange("p (b v) -> p b v", b=NB),
                                   r_vt[0:NSAMP, CK * P:].unsqueeze(1).broadcast_to([NSAMP, NB, P]),
                                   bmask[0:NSAMP, :].unsqueeze(2).broadcast_to([NSAMP, NB, P]),
                                   ALU.mult).then_inc(pool_rec, 1)

            spread_v(0)
            with pool.Fori(1, KT) as h:
                spread_v(h)

        @block.tensor
        def _(pe):
            pe.wait_ge(pool_ev.sem, pool_ev.at(0, "ones"))
            pe.wait_ge(vec_in, 5 * 16)
            nc.tensor.transpose(bank[7][:, 0:65], st_vec[0:65, :], ident[0:65, 0:65]).then_inc(K_PE, 1)
            pe.wait_ge(cst_in, 16)
            for k in range(KT):
                mm = nc.tensor.transpose(bank[6][:, k * 16:(k + 1) * 16], st_row[0:16, k * P:(k + 1) * P],
                                         ident[0:16, 0:16])
                if k < NCH:
                    mm.then_inc(bank_free[k], 1)
            mm.then_inc(K_PE, 1)
            pe.wait_ge(K_DVE, 2)
            pairs = ((3, 4), (5, 6))
            for i in range(9):
                r = P if i < 8 else NSAMP
                pe.wait_ge(S_DN.sem, S_DN.at(i, "xn"))
                if i >= 2:
                    pe.wait_ge(S_DT.sem, S_DT.at(i - 2, "tb"))
                for half in range(2):
                    for k in range(4):
                        kk = half * 4 + k
                        mm = nc.tensor.transpose(bank[pairs[i % 2][half]][:, k * P:k * P + r],
                                                 st_n[i % 2][0:r, kk * P:(kk + 1) * P], ident[0:r, 0:r])
                    mm.then_inc(S_PE.now("ta" if half == 0 else "tb"), 1)

            def group(b, w, src, c, use):
                pe.wait_ge(bank_free[b], emptied(use))
                for k in range(KT):
                    rhs = [s[:, k, c * CH:(c + 1) * CH] for s in src]
                    for i, (wi, hi) in enumerate(((0, 0), (1, 0), (0, 1))):
                        mm = nc.tensor.matmul(bank[b][:, 0:CH], w[wi][:, k, :], rhs[hi],
                                              start=(k == 0 and i == 0), stop=(k == KT - 1 and i == 2))
                mm.then_inc(proj_done, 1)

            def slot(i):
                return [wsplit[:, i, 0], wsplit[:, i, 1]]

            h0, o0 = halves(reg_a), halves(reg_b)
            with pe.Fori(0, KT) as j:
                for t in range(4):
                    pe.wait_ge(w_lo, j * 4 + t + 1)
                    for c in range(NCH):
                        if t == 0:
                            pe.wait_ge(S_DT.sem, S_DT.at((2, 5, 8)[c], "lo"))
                        group(c, slot(t % 2), h0, c, j * 4 + t)
            pe.wait_ge(C_DVE.sem, C_DVE.at(KT - 1, "last"))
            for half in range(2):
                for k in range(4):
                    kk = half * 4 + k
                    mm = nc.tensor.transpose(bank[6 + half][0:18, k * P:(k + 1) * P],
                                             c_last[:, kk * 18:(kk + 1) * 18], ident[:, :])
                mm.then_inc(tail_pe, 1)

            def sum_squares(ev, name, sq):
                nc.tensor.matmul(bank[7][:, 0:CH], ones[:, :], sq, start=True, stop=True).then_inc(ev.now(name), 1)

            def residual(c, m):
                if m >= 4:
                    pe.wait_ge(V_PO.sem, V_PO.at(c, f"x{m - 4}"))
                elif c >= 1:
                    pe.wait_ge(V_PO.sem, V_PO.at(c - 1, f"x{m + 4}"))
                for s, (o, r) in enumerate(SUBS):
                    mm = nc.tensor.transpose(bank[3 + m % 4][:, o:o + r], o_x[0:r, s * D + m * P:s * D + (m + 1) * P],
                                             ident[0:r, 0:r])
                mm.then_inc(P_PO.now(f"xt{m}"), 1)

            def post_a(c, at):
                if at == 0:
                    pe.wait_ge(V_ACC.sem, V_ACC.at(c, f"a{KT - 1}"))
                    if c >= 1:
                        pe.wait_ge(A_PO.sem, A_PO.at(c - 1, "sd2"))
                    else:
                        pe.wait_ge(tail_act, 2)
                    sum_squares(P_PO, "ss1", o_acc)
                    pe.wait_ge(xr_in, 16 * 3 * (c + 1) + (16 if c == 2 else 0))
                    for m in range(4):
                        residual(c, m)
                if at == 3:
                    for m in range(4, KT):
                        residual(c, m)
                if at == 5:
                    pe.wait_ge(V_PO.sem, V_PO.at(c, f"a{KT - 1}"))
                    pe.wait_ge(A_PO.sem, A_PO.at(c, "sd1"))
                    sum_squares(P_PO, "ss2", o_acc2)

            for c in range(NCH):
                for m in range(KT):
                    if c == 0:
                        pe.wait_ge(w_lo, NW1 + m + 1)
                    if m == 0 and c == 0:
                        pe.wait_ge(C_DVE.sem, C_DVE.at(KT - 1, "l2"))
                    g = c * KT + m
                    group(g % 3, wout_tile(reg_a, m), o0, c, NW1 + g // 3)
                    if c >= 1:
                        post_a(c - 1, m)
            for at in (0, 3, 5):
                post_a(NCH - 1, at)

            h1, o1 = halves(reg_b), halves(reg_a)

            def tokens(c, n=P):
                return slice(c * P, c * P + n)

            def level(h, m):
                b = bank[3 + LEVELS.index(m) % 2]
                if m == 64:
                    for c in range(CK):
                        mm = nc.tensor.matmul(b[0:64, c * 64:(c + 1) * 64], r_K[:, tokens(c, 64)],
                                              r_Q[:, c * P + 64:(c + 1) * P], start=True, stop=True)
                else:
                    for c in range(CK):
                        rhs = r_Q[:, tokens(c)].rearrange("p (b two r) -> p b two r", two=2, r=m)[:, :, 1, :]
                        mm = nc.tensor.matmul(b[:, c * 64:(c + 1) * 64].rearrange("p (b r) -> p b r", r=m),
                                              r_K[:, tokens(c)], rhs, start=True, stop=True)
                    if m < NS:
                        rhs = r_Q[:, NP:].rearrange("p (b two r) -> p b two r", two=2, r=m)[:, :, 1, :]
                        mm = nc.tensor.matmul(bank[7][0:NSAMP, 0:NSAMP // 2].rearrange("p (b r) -> p b r", r=m),
                                              r_K[:, NP:], rhs, start=True, stop=True)
                mm.then_inc(PR.now(f"L{m}"), 1)

            def turn_output(h):
                pe.wait_ge(VR.sem, VR.at(h, "ons"))
                for c in range(CK):
                    nc.tensor.transpose(bank[5 + c // 4][:, tokens(c % 4)], r_kt[:, tokens(c)], ident[:, :])
                nc.tensor.transpose(bank[7][:, 256:256 + NSAMP], r_kt[0:NSAMP, CK * P:],
                                    ident[0:NSAMP, 0:NSAMP]).then_inc(ot_done, 1)

            def rec(h, s, last):
                if s == 0:
                    if last is not None:
                        turn_output(last)
                    pe.wait_ge(VR.sem, VR.at(h, "q1"))
                    for c in range(CK):
                        nc.tensor.matmul(bank[3 + c // 4][:, tokens(c % 4)], r_K[:, tokens(c)], r_q[:, tokens(c)],
                                         start=True, stop=True)
                    nc.tensor.matmul(bank[7][0:NSAMP, 0:NSAMP], r_K[:, NP:], r_q[:, NP:], start=True,
                                     stop=True).then_inc(PR.now("dg"), 1)
                elif s == 1:
                    for c in range(NCH):
                        pe.wait_ge(bank_free[c], emptied(NW2 + 2 + 4 * h))
                    if last is not None:
                        pe.wait_ge(o_rdy, last + 1)
                    pe.wait_ge(VR.sem, VR.at(h, "as"))
                    for c in range(CK):
                        nc.tensor.transpose(bank[5 + c // 4][:, tokens(c % 4)], r_vr[:, tokens(c)], ident[:, :])
                    nc.tensor.transpose(bank[7][0:NSAMP, 128:256], r_vr[:, NP:], ident[:, :]).then_inc(PR.now("vt"), 1)
                    level(h, 1)
                elif s == 2:
                    pe.wait_ge(VR.sem, VR.at(h, "c1"))
                    level(h, 2)
                elif s == 3:
                    pe.wait_ge(VR.sem, VR.at(h, "c2"))
                    level(h, 4)
                    nc.tensor.transpose(bank[7][0:NSAMP, 0:P], r_K[:, NP:], ident[:, :]).then_inc(PR.now("kst"), 1)
                elif s == 4:
                    pe.wait_ge(AR.sem, AR.at(h, "kts"))
                    pe.wait_ge(s0_in, h * 16 + 16)
                    pe.wait_ge(VR.sem, VR.at(h, "c4"))
                    level(h, 8)
                    nc.tensor.matmul(bank[7][0:NSAMP, 0:P], r_as[0:NSAMP, :], r_vt[0:NSAMP, CK * P:],
                                     start=True, stop=False)
                    for b in range(NB):
                        mm = nc.tensor.matmul(bank[7][0:NSAMP, 0:P], r_qb[:, b * NSAMP:(b + 1) * NSAMP], r_s[:, tokens(b)],
                                              start=False, stop=(b == NB - 1))
                    mm.then_inc(PR.now("os"), 1)
                elif s == 5:
                    pe.wait_ge(VR.sem, VR.at(h, "c8"))
                    level(h, 16)
                    pe.wait_ge(pool_rec, h + 1)
                    pe.wait_ge(AR.sem, AR.at(h, "vt"))
                    for half in range(2):
                        mm = nc.tensor.matmul(bank[5 + half][:, :], r_kt[0:NSAMP, CK * P:],
                                              r_kt[0:NSAMP, half * 512:(half + 1) * 512], start=True, stop=True)
                    mm.then_inc(PR.now("us"), 1)
                elif s == 6:
                    pe.wait_ge(VR.sem, VR.at(h, "c16"))
                    level(h, 32)
                elif s == 7:
                    pe.wait_ge(VR.sem, VR.at(h, "c32"))
                    level(h, 64)
                elif s == 8:
                    pe.wait_ge(VR.sem, VR.at(h, "w64"))
                    for c in range(CK):
                        mm = nc.tensor.transpose(bank[5 + c // 4][:, tokens(c % 4)], r_K[:, tokens(c)], ident[:, :])
                    mm.then_inc(PR.now("kt"), 1)
                elif s == 9:
                    pe.wait_ge(AR.sem, AR.at(h, "kt"))
                    for c in range(CK):
                        mm = nc.tensor.matmul(bank[5 + c // 4][:, tokens(c % 4)], r_kt[:, tokens(c)], r_vt[:, tokens(c)],
                                              start=True, stop=True)
                    mm.then_inc(PR.now("u"), 1)
                elif s == 10:
                    pe.wait_ge(VR.sem, VR.at(h, f"s{CK - 1}"))
                    for c in range(CK):
                        dst = bank[3 + c // 4][:, tokens(c % 4)]
                        mm = nc.tensor.matmul(dst, r_am[:, tokens(c)], r_vt[:, tokens(c)], start=True, stop=(c == 0))
                        if c:
                            mm = nc.tensor.matmul(dst, r_Q[:, tokens(c)], r_s[:, tokens(c - 1)], start=False, stop=True)
                        if c % 4 == 3:
                            mm.then_inc(PR.now(f"o{c // 4}"), 1)

            def tile(n, s, use):
                pe.wait_ge(w_lo, n + 1)
                for c in range(NCH):
                    yield lambda c=c: group(c, slot(s), h1, c, use)

            for i in range(3):
                for c, run in enumerate(tile(NW2 + i, i % 2, NW2 + i)):
                    if i == 0:
                        pe.wait_ge(V_PO.sem, V_PO.at(c, f"l{KT - 1}"))
                    run()

            def iteration(j, last, tiles=(0, 1, 2, 3), n=None, use=None):
                base = NW2 - 1 + 4 * j
                for t in range(4):
                    runs = list(tile(base + t if n is None else n, (1 + t) % 2 if n is None else 1,
                                     base + t if use is None else use)) if t in tiles else None
                    for c in range(NCH):
                        if runs:
                            runs[c]()
                        rec(j - 1, 3 * t + c, last)

            iteration(1, None)
            with pe.Fori(2, KT) as j:
                iteration(j, j - 2)
            iteration(KT, KT - 2, (1,), NW3 - 1, NW3 - 1)
            turn_output(KT - 1)

            def post_b(c, at):
                if at == 0:
                    pe.wait_ge(V_ACC.sem, V_ACC.at(NCH + c, f"a{KT - 1}"))
                    if c >= 1:
                        pe.wait_ge(A_P2.sem, A_P2.at(c - 1, "sd1"))
                    sum_squares(P_P2, "ss1", o_acc)
                if at in (5, 6, 7):
                    s = at - 5
                    o, r = SUBS[s]
                    pe.wait_ge(V_P2.sem, V_P2.at(c, f"x{KT - 1}"))
                    if s == 2:
                        pe.wait_ge(A_P2.sem, A_P2.at(c, "y0"))
                    elif c:
                        pe.wait_ge(A_P2.sem, A_P2.at(c - 1, "y2" if s == 0 else "y1"))
                    for m in range(KT):
                        mm = nc.tensor.transpose(bank[3 + 2 * (s % 2) + m // 4][0:r, (m % 4) * P:(m % 4 + 1) * P],
                                                 o_y[c % 2][:, m, o:o + r], ident[:, :])
                    mm.then_inc(P_P2.now(f"y{s}"), 1)

            pe.wait_ge(o_lo, KT)
            for c in range(NCH):
                for m in range(KT):
                    if c == 0:
                        pe.wait_ge(w_lo, NW3 + m + 1)
                    g = c * KT + m
                    group(g % 3, wout_tile(reg_b, m), o1, c, NW3 + g // 3)
                    if c >= 1:
                        post_b(c - 1, m)
            for at in (0, 5, 6, 7):
                post_b(NCH - 1, at)

        @block.scalar
        def _(act):
            A = nc.scalar.activation

            def split_hi(s, half, used, dst=None):
                act.wait_ge(w_in_s[s], half * 16)
                act.wait_ge(proj_done, used)
                A(wsplit[:, s, 0] if dst is None else dst, wraw[:, s], ACT.Copy).then_inc(w_hi, 1)

            act.wait_ge(K_DVE, 3)
            A(st_lb[:, 1], st_lb[:, 0], ACT.Exp).then_inc(K_ACT, 1)

            def normalise(i):
                r = P if i < 8 else NSAMP
                act.wait_ge(x_in[i % 3], 16 * (i // 3 + 1))
                if i:
                    act.wait_ge(S_AN.sem, S_AN.at(i - 1, "sq"))
                A(st_scr[0:r, :], st_x[i % 3][0:r, :], ACT.Square,
                  accum_out=small[0:r, i:i + 1]).then_inc(S_AN.now("sq"), 1)
                act.wait_ge(S_AN.sem, S_AN.at(i, "sq"))
                A(small[0:r, 16 + i:17 + i], small[0:r, i:i + 1], ACT.Sqrt, bias=eps[0:r, :],
                  scale=1.0 / D).then_inc(S_AN.now("sd"), 1)

            normalise(0)
            for i in range(9):
                r = P if i < 8 else NSAMP
                if i < 8:
                    normalise(i + 1)
                act.wait_ge(S_DT.sem, S_DT.at(i, "tb"))
                A(halves(reg_a)[0][:, :, i * P:i * P + r], st_t[i % 2].rearrange("p (k t) -> p k t", k=KT)[:, :, 0:r],
                  ACT.Copy).then_inc(S_AT.now("hi"), 1)
                if i == 2:
                    split_hi(0, 1, 0)
            act.wait_ge(S_DT.sem, S_DT.at(8, "lo"))

            with act.Fori(0, KT) as j:
                for t in range(4):
                    n3 = 12 * j + 3 * t
                    split_hi((t + 1) % 2, j * 2 + ((t + 1) // 2 + 1), n3 + 1)
                    if t == 0:
                        for c in range(NCH):
                            act.wait_ge(proj_done, n3 + (c + 1))
                            A(c_v[:, c * CH:(c + 1) * CH], bank[c][:, 0:CH], ACT.Copy).then_inc(bank_free[c], 1)
                    if t == 3:
                        for c in range(NCH):
                            act.wait_ge(proj_done, n3 + (c + 1))
                            A(c_g[:, c * CH:(c + 1) * CH], bank[c][:, 0:CH], ACT.Sigmoid).then_inc(C_ACT.now(f"g{c}"), 1)
                        for c in range(NCH):
                            act.wait_ge(C_DVE.sem, C_DVE.at(j, f"o{c}"))
                            A(reg_b[:, bass.ds(j * T + c * CH, CH)], c_o[:, c * CH:(c + 1) * CH],
                              ACT.Copy).then_inc(C_ACT.now(f"h{c}"), 1)
            for half in range(2):
                act.wait_ge(tail_pe, 2)
                A(c_last18[0:18, half * 512:(half + 1) * 512], bank[6 + half][0:18, :], ACT.Copy).then_inc(tail_act, 1)

            def out_evac(base, rnd, c, m):
                g = c * KT + m
                if rnd * KT + m >= 2:
                    prev = rnd * KT + m - 2
                    act.wait_ge(V_ACC.sem, V_ACC.at(prev // KT, f"a{prev % KT}"))
                act.wait_ge(proj_done, base + g + 1)
                A(o_sq[m % 2], bank[g % 3][:, 0:CH], ACT.Square).then_inc(A_SQ.now(f"sq{m}"), 1)
                A(o_y[c % 2][:, m], bank[g % 3][:, 0:CH], ACT.Copy).then_inc(bank_free[g % 3], 1)

            def root(ev, ev_pe, c, name, pe_name):
                act.wait_ge(ev_pe.sem, ev_pe.at(c, pe_name))
                A(o_rb, bank[7][:, 0:CH], ACT.Sqrt, bias=eps[:, :], scale=1.0 / D).then_inc(ev.now(name), 1)

            def post_a(c, at):
                if at == 0:
                    root(A_PO, P_PO, c, "sd1", "ss1")
                for m in {1: (0, 1), 2: (2, 3), 4: (4, 5, 6, 7)}.get(at, ()):
                    act.wait_ge(V_PO.sem, V_PO.at(c, f"x{m}"))
                    if m:
                        act.wait_ge(V_PO.sem, V_PO.at(c, f"a{m - 1}"))
                    A(o_t2, o_y[c % 2][:, m], ACT.Square).then_inc(A_PO.now(f"s{m}"), 1)
                if at == 5:
                    root(A_PO, P_PO, c, "sd2", "ss2")
                for m in {6: (0, 1, 2, 3), 7: (4, 5, 6, 7)}.get(at, ()):
                    act.wait_ge(V_PO.sem, V_PO.at(c, f"u{m}"))
                    A(halves(reg_b)[0][:, m, c * CH:(c + 1) * CH], o_t[m % 2], ACT.Copy,
                      scale=cst[:, PRE + KT + m:PRE + KT + m + 1]).then_inc(A_PO.now(f"h{m}"), 1)

            act.wait_ge(C_DVE.sem, C_DVE.at(KT - 1, "l2"))
            for c in range(NCH):
                for m in range(KT):
                    if c == 0 and m < KT - 1:
                        n = NW1 + m + 1
                        split_hi(n % 2, n // 2 + 1, G_OUT1, wout_tile(reg_a, m + 1)[0])
                    if c == 2 and m == 0:
                        act.wait_ge(spill[0], 16)
                    out_evac(G_OUT1, c, c, m)
                    if c == 2 and m < 2:
                        split_hi(m, (NW2 + m) // 2 + 1, out_use(G_OUT1, m))
                    if c:
                        post_a(c - 1, m)
            for at in range(KT):
                post_a(NCH - 1, at)
            act.wait_ge(V_PO.sem, V_PO.at(2, f"l{KT - 1}"))
            act.wait_ge(spill[1], 16)

            def turn_hi(h):
                act.wait_ge(o_rdy, h + 1)
                A(reg_a[:, bass.ds(h * T, T)], r_o, ACT.Copy).then_inc(o_hi, 1)

            states = r_s.rearrange("p (b v) -> p b v", b=NB)

            def rec(h, s, last):
                if s == 1:
                    if last is None:
                        act.wait_ge(P_PO.sem, P_PO.at(2, f"xt{KT - 1}"))
                    else:
                        act.wait_ge(sp_out, h * 16)
                    act.dma_start(states, state_hgrn[0, :, bass.ds(h, 1)].rearrange("b h k v -> k (b h) v")).then_inc(s0_in, 16)
                    act.wait_ge(PR.sem, PR.at(h, "vt"))
                    for half in range(2):
                        ins = A(r_vt[:, half * 512:(half + 1) * 512], bank[5 + half][:, :], ACT.Copy)
                    ins.then_inc(AR.now("vt"), 1)
                    if last is not None:
                        turn_hi(last)
                elif s == 3:
                    act.wait_ge(PR.sem, PR.at(h, "kst"))
                    A(r_kt[0:NSAMP, CK * P:], bank[7][0:NSAMP, 0:P], ACT.Copy).then_inc(AR.now("kts"), 1)
                elif s == 4:
                    act.wait_ge(PR.sem, PR.at(h, "os"))
                    A(r_os[0:NSAMP, :], bank[7][0:NSAMP, 0:P], ACT.Copy).then_inc(AR.now("os"), 1)
                    act.wait_ge(AR.sem, AR.at(h, "os"))
                    A(bank[7][0:NSAMP, P:2 * P], r_os[0:NSAMP, :], ACT.Square,
                      accum_out=small[0:NSAMP, CK:CK + 1]).then_inc(AR.now("sqs"), 1)
                elif s == 6:
                    act.wait_ge(VR.sem, VR.at(h, "snew"))
                    act.dma_start(hgrn_s[0, :, bass.ds(h, 1)].rearrange("b h k v -> k (b h) v"), states).then_inc(s0_out, 16)
                elif s == 8:
                    act.wait_ge(PR.sem, PR.at(h, "kt"))
                    for half in range(2):
                        ins = A(r_kt[:, half * 512:(half + 1) * 512], bank[5 + half][:, :], ACT.Copy)
                    ins.then_inc(AR.now("kt"), 1)
                elif s == 10:
                    act.wait_ge(PR.sem, PR.at(h, "o1"))
                    for half in range(2):
                        A(r_sq[:, half * 512:(half + 1) * 512], bank[3 + half][:, :], ACT.Square).then_inc(AR.now(f"sq{half}"), 1)
                    act.wait_ge(VR.sem, VR.at(h, "r1"))
                    A(small[:, 16:16 + CK], small[:, 0:CK], ACT.Sqrt, bias=eps[:, :], scale=1.0 / P).then_inc(AR.now("sd"), 1)
                    A(small[0:NSAMP, 16 + CK:17 + CK], small[0:NSAMP, CK:CK + 1], ACT.Sqrt, bias=eps[0:NSAMP, :],
                      scale=1.0 / P).then_inc(AR.now("sds"), 1)
                    act.wait_ge(VR.sem, VR.at(h, f"s{CK - 1}"))
                    act.dma_start(hgrn_p[0, 0, bass.ds(h, 1)].rearrange("h k v -> k (h v)"),
                                  r_s[:, (CK - 1) * P:]).then_inc(sp_out, 16)

            def evac(kind, c, done, h):
                act.wait_ge(proj_done, done)
                src = bank[c][:, 0:CH]
                cols = slice(c * CH, (c + 1) * CH)
                if kind == "q":
                    if h is not None and c == 0:
                        act.wait_ge(PR.sem, PR.at(h, "dg"))
                    A(r_q[:, cols], src, ACT.Sigmoid).then_inc(q_sig, 1)
                elif kind == "z":
                    A(r_g[:, cols], src, ACT.Sigmoid).then_inc(z_sig, 1)
                elif kind == "v":
                    A(r_vr[:, cols], src, ACT.Copy).then_inc(bank_free[c], 1)
                else:
                    A(r_f[:, cols], src, ACT.Sigmoid)
                    A(r_kr[:, cols], src, ACT.Sigmoid, scale=-1.0).then_inc(bank_free[c], 1)

            for i, kind in enumerate("qvf"):
                n = NW2 + i + 1
                if i:
                    split_hi(n % 2, n // 2 + 1, G_IN2 + 3 * i)
                for c in range(NCH):
                    evac(kind, c, G_IN2 + 3 * i + c + 1, None)

            def iteration(j, last):
                for t, kind in enumerate("qzvf"):
                    for c in range(NCH):
                        if c == 0:
                            split_hi(t % 2, 2 * j + (NW2 + t) // 2 + 1, G_IN2 - 3 + 3 * t + 12 * j)
                        evac(kind, c, G_IN2 - 3 + 3 * t + c + 1 + 12 * j, j - 1)
                        rec(j - 1, 3 * t + c, last)

            iteration(1, None)
            with act.Fori(2, KT) as j:
                iteration(j, j - 2)
            split_hi(0, NW3 // 2 + 1, G_OUT2 - 3)
            for s in range(12):
                if 3 <= s < 6:
                    evac("z", s - 3, G_OUT2 - 3 + s - 2, None)
                rec(KT - 1, s, KT - 2)
                if s >= 5:
                    m = s - 4
                    split_hi(m % 2, (NW3 + m) // 2 + 1, G_OUT2, wout_tile(reg_b, m)[0])
            turn_hi(KT - 1)
            act.wait_ge(o_lo, KT)

            def post_b(c, at):
                if at == 0:
                    root(A_P2, P_P2, c, "sd1", "ss1")
                if at >= 5:
                    s = at - 5
                    r = SUBS[s][1]
                    act.wait_ge(P_P2.sem, P_P2.at(c, f"y{s}"))
                    if c or s:
                        act.wait_ge(yout, 16 * (3 * c + s))
                    for half in range(2):
                        ins = A(o_yt[0:r, half * 512:(half + 1) * 512], bank[3 + 2 * (s % 2) + half][0:r, :], ACT.Copy)
                    ins.then_inc(A_P2.now(f"y{s}"), 1)

            for c in range(NCH):
                for m in range(KT):
                    out_evac(G_OUT2, NCH + c, c, m)
                    if c:
                        post_b(c - 1, m)
            for at in range(KT):
                post_b(NCH - 1, at)

        @block.vector
        def _(dve):
            V = nc.vector

            def split_lo(count, s, dst=None, hi=None):
                dve.wait_ge(w_hi, count)
                d, h = (wsplit[:, s, 1], wsplit[:, s, 0]) if dst is None else (dst, hi)
                V.tensor_tensor(d, wraw[:, s], h.bitcast(F32), ALU.subtract).then_inc(w_lo, 1)

            V.memset(eps[:, :], EPS)
            dve.wait_ge(K_PE, 1)
            V.tensor_copy(cst[:, :], bank[7][:, 0:65]).then_inc(K_DVE, 1)
            dve.wait_ge(K_PE, 2)
            V.tensor_copy(c_st, bank[6][:, 0:KT * 16]).then_inc(K_DVE, 1)
            dve.wait_ge(K_DVE, 2)
            V.tensor_tensor(st_lb[:, 0], cst[:, LBL:LBL + KT], cst[:, LBL:LBL + KT], ALU.subtract).then_inc(K_DVE, 1)
            dve.wait_ge(K_ACT, 1)
            V.reciprocal(st_lb[:, 2], st_lb[:, 1]).then_inc(K_DVE, 1)
            dve.wait_ge(K_DVE, 4)
            V.tensor_tensor(st_lb[:, 3], st_lb[:, 1], st_lb[:, 2], ALU.mult).then_inc(K_DVE, 1)
            dve.wait_ge(K_DVE, 5)
            V.tensor_tensor(lb[:, 0], st_lb[:, 3], st_lb[:, 3], ALU.subtract).then_inc(K_DVE, 1)
            dve.wait_ge(K_DVE, 6)
            V.tensor_scalar(lb[:, 1], lb[:, 0], -1.0, 1.0, ALU.mult, ALU.add).then_inc(K_DVE, 1)

            def normalise(i):
                r = P if i < 8 else NSAMP
                dve.wait_ge(S_AN.sem, S_AN.at(i, "sd"))
                V.reciprocal(small[0:r, 32 + i:33 + i], small[0:r, 16 + i:17 + i]).then_inc(S_DN.now("rs"), 1)
                dve.wait_ge(S_DN.sem, S_DN.at(i, "rs"))
                if i >= 2:
                    dve.wait_ge(S_PE.sem, S_PE.at(i - 2, "tb"))
                V.tensor_scalar(st_n[i % 2][0:r, :], st_x[i % 3][0:r, :], small[0:r, 32 + i:33 + i], None,
                                ALU.mult).then_inc(S_DN.now("xn"), 1)

            normalise(0)
            h_hi, h_lo = halves(reg_a)
            for i in range(9):
                r = P if i < 8 else NSAMP
                if i < 8:
                    normalise(i + 1)
                dst = st_t[i % 2].rearrange("p (k t) -> p k t", k=KT)
                if i >= 2:
                    dve.wait_ge(S_AT.sem, S_AT.at(i - 2, "hi"))
                for half, name in enumerate(("ta", "tb")):
                    dve.wait_ge(S_PE.sem, S_PE.at(i, name))
                    src = bank[((3, 4), (5, 6))[i % 2][half]][:, :].rearrange("p (k t) -> p k t", k=4)[:, :, 0:r]
                    g = cst[:, PRE + 4 * half:PRE + 4 * half + 4].unsqueeze(2).broadcast_to([P, 4, r])
                    V.tensor_tensor(dst[:, 4 * half:4 * half + 4, 0:r], src, g, ALU.mult).then_inc(S_DT.now(name), 1)
                dve.wait_ge(S_AT.sem, S_AT.at(i, "hi"))
                V.tensor_tensor(h_lo[:, :, i * P:i * P + r], dst[:, :, 0:r],
                                h_hi[:, :, i * P:i * P + r].bitcast(F32), ALU.subtract).then_inc(S_DT.now("lo"), 1)
                if i == 2:
                    split_lo(1, 0)
            dve.wait_ge(pool_ev.sem, pool_ev.at(0, "qb0"))
            for i, m in enumerate(LEVELS[:-1]):
                V.tensor_copy(masks[m][:, :], st_ms[:, 64 * i:64 * i + 64])

            V.memset(c_u[:, 0:2], 0.0)
            us = c_u[:, UL:].rearrange("p (b s) -> p b s", b=NB)
            accs = c_acc[:, NP:].rearrange("p (b s) -> p b s", b=NB)
            with dve.Fori(0, KT) as j:
                for t in range(4):
                    n3 = 12 * j + 3 * t
                    split_lo(4 * j + (t + 2), (t + 1) % 2)
                    if t == 0:
                        V.tensor_copy(us[:, :, 0:2], c_st[:, bass.ds(j * 2 * NB, 2 * NB)]
                                      .rearrange("p (b w) -> p b w", b=NB)).then_inc(C_DVE.now("st"), 1)
                        for w in range(3):
                            ins = V.tensor_copy(c_w[:, w:w + 1], cst[:, bass.ds(j + CW + w * KT, 1)])
                        ins.then_inc(C_DVE.now("cw"), 1)
                    if t == 1:
                        for c in range(NCH):
                            dve.wait_ge(proj_done, n3 + (c + 1))
                            dve.wait_ge(bank_free[c], emptied(4 * j + 1))
                            a, b = c * CH, min((c + 1) * CH, NP)
                            ins = V.tensor_tensor(c_u[:, 2 + a:2 + b], bank[c][:, 0:b - a], c_v[:, a:b], ALU.mult)
                            if c == NCH - 1:
                                ins = V.tensor_tensor(us[:, :, 2:], bank[c][:, b - a:CH].rearrange("p (b s) -> p b s", b=NB),
                                                      c_v[:, b:].rearrange("p (b s) -> p b s", b=NB), ALU.mult)
                            ins.then_inc(bank_free[c], 1)
                        dve.wait_ge(C_DVE.sem, C_DVE.at(j, "cw"))
                        for c in range(NCH):
                            dve.wait_ge(bank_free[c], emptied(4 * j + 2))
                        V.tensor_scalar(c_acc[:, 0:NP], c_u[:, 0:NP], c_w[:, 0:1], None, ALU.mult)
                        V.tensor_scalar(accs, us[:, :, 0:NS], c_w[:, 0:1], None, ALU.mult).then_inc(C_DVE.now("a0"), 1)
                        for w in (1, 2):
                            dve.wait_ge(C_DVE.sem, C_DVE.at(j, f"a{w - 1}"))
                            V.scalar_tensor_tensor(c_acc[:, 0:NP], c_u[:, w:w + NP], c_w[:, w:w + 1], c_acc[:, 0:NP],
                                                   ALU.mult, ALU.add)
                            V.scalar_tensor_tensor(accs, us[:, :, w:w + NS], c_w[:, w:w + 1], accs, ALU.mult,
                                                   ALU.add).then_inc(C_DVE.now(f"a{w}"), 1)
                        V.tensor_copy(c_last[:, bass.ds(j * 18, 2)], c_u[:, NP:NP + 2])
                        V.tensor_copy(c_last[:, bass.ds(j * 18 + 2, 16)].rearrange("p (b w) -> p b w", b=NB),
                                      us[:, :, NS:]).then_inc(C_DVE.now("last"), 1)
                    if t == 2:
                        dve.wait_ge(C_DVE.sem, C_DVE.at(j, "a2"))
                        for c in range(NCH):
                            dve.wait_ge(proj_done, n3 + (c + 1))
                            cols = slice(c * CH, (c + 1) * CH)
                            V.tensor_tensor(c_acc[:, cols], bank[c][:, 0:CH], c_acc[:, cols], ALU.mult).then_inc(bank_free[c], 1)
                    if t == 3:
                        for c in range(NCH):
                            dve.wait_ge(C_ACT.sem, C_ACT.at(j, f"g{c}"))
                            cols = slice(c * CH, (c + 1) * CH)
                            V.tensor_tensor(c_g[:, cols], bank[c][:, 0:CH], c_g[:, cols], ALU.mult).then_inc(bank_free[c], 1)
                            dve.wait_ge(bank_free[c], emptied(4 * j + 4))
                            V.tensor_tensor(c_o[:, cols], c_acc[:, cols], c_g[:, cols], ALU.mult).then_inc(C_DVE.now(f"o{c}"), 1)
                        for c in range(NCH):
                            dve.wait_ge(C_ACT.sem, C_ACT.at(j, f"h{c}"))
                            V.tensor_tensor(reg_b[:, bass.ds(KT * T + c * CH + j * T, CH)], c_o[:, c * CH:(c + 1) * CH],
                                            reg_b[:, bass.ds(j * T + c * CH, CH)].bitcast(F32),
                                            ALU.subtract).then_inc(C_DVE.now(f"l{c}"), 1)

            def add_square(rnd, m, ev_pe, c):
                dve.wait_ge(A_SQ.sem, A_SQ.at(rnd, f"sq{m}"))
                if m:
                    dve.wait_ge(V_ACC.sem, V_ACC.at(rnd, f"a{m - 1}"))
                    V.tensor_tensor(o_acc, o_acc, o_sq[m % 2], ALU.add).then_inc(V_ACC.now(f"a{m}"), 1)
                else:
                    if c:
                        dve.wait_ge(ev_pe.sem, ev_pe.at(c - 1, "ss1"))
                    V.tensor_copy(o_acc, o_sq[0]).then_inc(V_ACC.now("a0"), 1)

            def inv(ev, ev_act, c, name, act_name):
                dve.wait_ge(ev_act.sem, ev_act.at(c, act_name))
                V.reciprocal(o_rb, o_rb).then_inc(ev.now(name), 1)

            def acc2(c, m):
                dve.wait_ge(A_PO.sem, A_PO.at(c, f"s{m}"))
                if m:
                    dve.wait_ge(V_PO.sem, V_PO.at(c, f"a{m - 1}"))
                    V.tensor_tensor(o_acc2, o_acc2, o_t2, ALU.add).then_inc(V_PO.now(f"a{m}"), 1)
                else:
                    if c:
                        dve.wait_ge(P_PO.sem, P_PO.at(c - 1, "ss2"))
                    V.tensor_copy(o_acc2, o_t2).then_inc(V_PO.now("a0"), 1)

            def lo_next(c, m):
                dve.wait_ge(A_PO.sem, A_PO.at(c, f"h{m}"))
                cols = slice(c * CH, (c + 1) * CH)
                hh, hl = halves(reg_b)
                V.scalar_tensor_tensor(hl[:, m, cols], o_t[m % 2], cst[:, PRE + KT + m:PRE + KT + m + 1],
                                       hh[:, m, cols].bitcast(F32), ALU.mult, ALU.subtract).then_inc(V_PO.now(f"l{m}"), 1)

            def post_a(c, at):
                y = o_y[c % 2]
                if at == 0:
                    if c == 0:
                        dve.wait_ge(cout, 32)
                    inv(V_PO, A_PO, c, "rb1", "sd1")
                for m in {1: (0, 1), 2: (2, 3), 4: (4, 5, 6, 7)}.get(at, ()):
                    dve.wait_ge(V_PO.sem, V_PO.at(c, f"x{m - 2}" if m >= 2 else "rb1"))
                    V.tensor_tensor(o_t[m % 2], y[:, m], o_rb, ALU.mult).then_inc(V_PO.now(f"t{m}"), 1)
                    dve.wait_ge(V_PO.sem, V_PO.at(c, f"t{m}"))
                    dve.wait_ge(P_PO.sem, P_PO.at(c, f"xt{m}"))
                    V.scalar_tensor_tensor(y[:, m], o_t[m % 2], cst[:, POST + m:POST + m + 1], bank[3 + m % 4][:, 0:CH],
                                           ALU.mult, ALU.add).then_inc(V_PO.now(f"x{m}"), 1)
                    if m:
                        acc2(c, m - 1)
                if at == 4:
                    acc2(c, KT - 1)
                if at == 6:
                    inv(V_PO, A_PO, c, "rb2", "sd2")
                for m in {6: (0, 1, 2, 3), 7: (4, 5, 6, 7)}.get(at, ()):
                    dve.wait_ge(V_PO.sem, V_PO.at(c, f"l{m - 2}" if m >= 2 else "rb2"))
                    V.tensor_tensor(o_t[m % 2], y[:, m], o_rb, ALU.mult).then_inc(V_PO.now(f"u{m}"), 1)
                    if m:
                        lo_next(c, m - 1)
                if at == 7:
                    lo_next(c, KT - 1)

            for c in range(NCH):
                for m in range(KT):
                    if c == 0 and m < KT - 1:
                        hi, lo = wout_tile(reg_a, m + 1)
                        split_lo(NW1 + m + 2, (m + 1) % 2, lo, hi)
                    add_square(c, m, P_PO, c)
                    if c == 2 and m < 2:
                        split_lo(NW2 + m + 1, m)
                    if c:
                        post_a(c - 1, m)
            for at in range(KT):
                post_a(NCH - 1, at)

            def pairs(ap, m):
                v = ap.rearrange("p (b two r) -> p b two r", two=2, r=m)
                return v[:, :, 0, :], v[:, :, 1, :]

            def level(h, m):
                dve.wait_ge(VR.sem, VR.at(h, "as" if m == 1 else f"u{m // 2}"))
                dve.wait_ge(PR.sem, PR.at(h, f"L{m}"))
                n = T if m < NS else NP
                nb = n // (2 * m)
                kl, _ = pairs(r_K[:, 0:n], m)
                _, qr = pairs(r_Q[:, 0:n], m)
                if m == 1:
                    fl, fr = pairs(r_f[:, 0:n], 1)
                    tl, tr = fl[:, :, 0], fr[:, :, 0]
                    tot = r_tt[:, :]
                else:
                    tt = r_tt[:, 0:n // 2].rearrange("p (b two r) -> p b two r", two=2, r=m // 2)[:, :, :, 0]
                    tl, tr = tt[:, :, 0], tt[:, :, 1]
                    tot = tl
                V.tensor_tensor(qr, qr, tl.unsqueeze(2).broadcast_to([P, nb, m]), ALU.mult)
                V.tensor_tensor(kl, kl, tr.unsqueeze(2).broadcast_to([P, nb, m]), ALU.mult).then_inc(VR.now(f"w{m}"), 1)
                b = bank[3 + LEVELS.index(m) % 2]
                if m == 64:
                    dst = r_am[0:64, :].rearrange("p (c t) -> p c t", c=CK)[:, :, 64:]
                    ins = V.tensor_copy(dst, b[0:64, :].rearrange("p (c t) -> p c t", c=CK))
                else:
                    dst = r_am.rearrange("p (c b two r) -> p c b two r", c=CK, two=2, r=m)[:, :, :, 1, :]
                    shape = [P, CK, 64 // m, m]
                    mask = masks[m][:, :].rearrange("p (b r) -> p b r", r=m)
                    ins = V.copy_predicated(dst, mask.unsqueeze(1).broadcast_to(shape),
                                            b[:, :].rearrange("p (c b r) -> p c b r", c=CK, r=m))
                if m < NS:
                    _, dst = pairs(r_as[:, :], m)
                    ins = V.copy_predicated(dst, mask[0:NSAMP, 0:NSAMP // (2 * m)],
                                            bank[7][0:NSAMP, 0:NSAMP // 2].rearrange("p (b r) -> p b r", r=m))
                ins.then_inc(VR.now(f"c{m}"), 1)
                dve.wait_ge(VR.sem, VR.at(h, f"w{m}"))
                V.tensor_tensor(tot, tl, tr, ALU.mult).then_inc(VR.now(f"u{m}"), 1)

            def prepare(h):
                V.tensor_copy(lbh[:, :].unsqueeze(2), lb[:, :, bass.ds(h, 1)]).then_inc(VR.now("lb"), 1)
                for c in range(NCH):
                    dve.wait_ge(bank_free[c], emptied(NW2 + 3 + 4 * h))
                dve.wait_ge(VR.sem, VR.at(h, "lb"))
                V.tensor_scalar(r_K, r_kr, lbh[:, 1:2], None, ALU.mult).then_inc(VR.now("k"), 1)
                V.tensor_scalar(r_f, r_f, lbh[:, 1:2], lbh[:, 0:1], ALU.mult, ALU.add).then_inc(VR.now("fa"), 1)
                dve.wait_ge(VR.sem, VR.at(h, "fa"))
                V.tensor_scalar(r_f, r_f, F_FLOOR, None, ALU.max).then_inc(VR.now("f"), 1)
                dve.wait_ge(VR.sem, VR.at(h, "f"))
                V.tensor_tensor(r_Q, r_q, r_f, ALU.mult).then_inc(VR.now("q1"), 1)

            def gate(h):
                dve.wait_ge(ot_done, h + 1)
                for a, b, src in ((0, 512, bank[5][:, :]), (512, NP, bank[6][:, :]), (NP, T, bank[7][:, 256:256 + NSAMP])):
                    ins = V.scalar_tensor_tensor(r_o[:, a:b], src, cst[:, ONRM:ONRM + 1], r_g[:, a:b], ALU.mult, ALU.mult)
                ins.then_inc(o_rdy, 1)

            def turn_lo(h):
                dve.wait_ge(o_hi, h + 1)
                V.tensor_tensor(reg_a[:, bass.ds(h * T + KT * T, T)], r_o, reg_a[:, bass.ds(h * T, T)].bitcast(F32),
                                ALU.subtract).then_inc(o_lo, 1)

            def rec(h, s, last):
                if s == 0:
                    dve.wait_ge(PR.sem, PR.at(h, "dg"))
                    for half in range(2):
                        ins = V.tensor_tensor(r_am[:, half * 512:(half + 1) * 512].rearrange("p (c t) -> p c t", c=4),
                                              bank[3 + half][:, :].rearrange("p (c t) -> p c t", c=4),
                                              ident[:, :].unsqueeze(1).broadcast_to([P, 4, P]), ALU.mult)
                    ins.then_inc(VR.now("am"), 1)
                    V.tensor_tensor(r_as[:, :], bank[7][0:NSAMP, 0:NSAMP], ident[0:NSAMP, 0:NSAMP],
                                    ALU.mult).then_inc(VR.now("as"), 1)
                    if last is not None:
                        gate(last)
                elif s == 1:
                    dve.wait_ge(PR.sem, PR.at(h, "L1"))
                    V.tensor_copy(r_vt[0:NSAMP, CK * P:], bank[7][0:NSAMP, P:2 * P]).then_inc(VR.now("vs"), 1)
                    level(h, 1)
                    if last is not None:
                        turn_lo(last)
                elif s == 2:
                    level(h, 2)
                    dve.wait_ge(VR.sem, VR.at(h, "w2"))
                    V.tensor_copy(r_qb[:, :].rearrange("p (b s) -> p b s", b=NB)[:, :, 0:NS],
                                  r_Q[:, NP:].rearrange("p (b s) -> p b s", b=NB)).then_inc(VR.now("qb"), 1)
                elif s <= 7:
                    level(h, 1 << (s - 1))
                    if s == 5:
                        dve.wait_ge(PR.sem, PR.at(h, "us"))
                        dve.wait_ge(VR.sem, VR.at(h, "u2"))
                        st = r_s.rearrange("p (b v) -> p b v", b=NB)
                        tot = r_tt[:, NP // 2:].rearrange("p (b two) -> p b two", two=2)[:, :, 0]
                        V.tensor_tensor(st, st, tot.unsqueeze(2).broadcast_to([P, NB, P]), ALU.mult).then_inc(VR.now("ss"), 1)
                        dve.wait_ge(VR.sem, VR.at(h, "ss"))
                        for half, name in enumerate(("sn0", "snew")):
                            V.tensor_tensor(r_s[:, half * 512:(half + 1) * 512], r_s[:, half * 512:(half + 1) * 512],
                                            bank[5 + half][:, :], ALU.add).then_inc(VR.now(name), 1)
                elif s == 9:
                    dve.wait_ge(PR.sem, PR.at(h, "u"))
                    dve.wait_ge(s0_out, h * 16 + 16)
                    for c in range(CK):
                        cols = slice(c * P, (c + 1) * P)
                        src = bank[5 + c // 4][:, (c % 4) * P:(c % 4 + 1) * P]
                        if c == 0:
                            ins = V.tensor_copy(r_s[:, cols], src)
                        else:
                            dve.wait_ge(VR.sem, VR.at(h, f"s{c - 1}"))
                            ins = V.scalar_tensor_tensor(r_s[:, cols], r_s[:, (c - 1) * P:c * P], r_tt[:, c * 64:c * 64 + 1],
                                                         src, ALU.mult, ALU.add)
                        ins.then_inc(VR.now(f"s{c}"), 1)
                elif s == 10:
                    for half in range(2):
                        dve.wait_ge(AR.sem, AR.at(h, f"sq{half}"))
                        V.tensor_reduce(small[:, 4 * half:4 * half + 4], r_sq[:, half * 512:(half + 1) * 512]
                                        .rearrange("p (c v) -> p c v", c=4), AX.X, ALU.add).then_inc(VR.now(f"r{half}"), 1)
                    dve.wait_ge(AR.sem, AR.at(h, "sd"))
                    V.reciprocal(small[:, 32:32 + CK], small[:, 16:16 + CK]).then_inc(VR.now("rs"), 1)
                    dve.wait_ge(AR.sem, AR.at(h, "sds"))
                    V.reciprocal(small[0:NSAMP, 32 + CK:33 + CK], small[0:NSAMP, 16 + CK:17 + CK]).then_inc(VR.now("rss"), 1)
                    dve.wait_ge(VR.sem, VR.at(h, "rss"))
                    for half in range(2):
                        V.tensor_tensor(r_kt[:, half * 512:(half + 1) * 512].rearrange("p (c v) -> p c v", c=4),
                                        bank[3 + half][:, :].rearrange("p (c v) -> p c v", c=4),
                                        small[:, 32 + 4 * half:36 + 4 * half].unsqueeze(2).broadcast_to([P, 4, P]),
                                        ALU.mult).then_inc(VR.now(f"on{half}"), 1)
                    V.tensor_scalar(r_kt[0:NSAMP, CK * P:], r_os[0:NSAMP, :], small[0:NSAMP, 32 + CK:33 + CK], None,
                                    ALU.mult).then_inc(VR.now("ons"), 1)

            def evac(kind, c, j):
                sig, buf = (q_sig, r_q) if kind == "q" else (z_sig, r_g)
                cols = slice(c * CH, (c + 1) * CH)
                dve.wait_ge(sig, 3 * j + (c + 1))
                V.scalar_tensor_tensor(buf[:, cols], buf[:, cols], QSCALE if kind == "q" else 1.0, bank[c][:, 0:CH],
                                       ALU.mult, ALU.mult).then_inc(bank_free[c], 1)

            for c in range(NCH):
                evac("q", c, 0)
            split_lo(NW2 + 3, 0)
            split_lo(NW2 + 4, 1)
            dve.wait_ge(spill[2], 16)

            def iteration(j, last):
                prepare(j - 1)
                for t, kind in enumerate("qzvf"):
                    for c in range(NCH):
                        if kind == "q":
                            evac("q", c, j)
                        elif kind == "z":
                            evac("z", c, j - 1)
                        rec(j - 1, 3 * t + c, last)
                        if c == 0:
                            split_lo(4 * j + (NW2 + t + 1), t % 2)

            iteration(1, None)
            with dve.Fori(2, KT) as j:
                iteration(j, j - 2)
            prepare(KT - 1)
            split_lo(NW3 + 1, 0)
            for s in range(12):
                if 3 <= s < 6:
                    evac("z", s - 3, KT - 1)
                rec(KT - 1, s, KT - 2)
                if s >= 5:
                    m = s - 4
                    hi, lo = wout_tile(reg_b, m)
                    split_lo(NW3 + m + 1, m % 2, lo, hi)
            gate(KT - 1)
            turn_lo(KT - 1)

            def x2(c, m):
                y = o_y[c % 2]
                dve.wait_ge(V_P2.sem, V_P2.at(c, f"t{m}"))
                V.scalar_tensor_tensor(y[:, m], o_t[m % 2], cst[:, POST + KT + m:POST + KT + m + 1], o_x1[:, m],
                                       ALU.mult, ALU.add).then_inc(V_P2.now(f"x{m}"), 1)

            def post_b(c, at):
                if at == 0:
                    inv(V_P2, A_P2, c, "rb1", "sd1")
                    dve.wait_ge(xr_in, 160 + 16 * (c + 1))
                for m in {1: (0, 1), 2: (2, 3), 3: (4, 5), 4: (6, 7)}.get(at, ()):
                    dve.wait_ge(V_P2.sem, V_P2.at(c, f"x{m - 2}" if m >= 2 else "rb1"))
                    V.tensor_tensor(o_t[m % 2], o_y[c % 2][:, m], o_rb, ALU.mult).then_inc(V_P2.now(f"t{m}"), 1)
                    if m:
                        x2(c, m - 1)
                if at == 4:
                    x2(c, KT - 1)

            for c in range(NCH):
                for m in range(KT):
                    add_square(NCH + c, m, P_P2, c)
                    if c:
                        post_b(c - 1, m)
            for at in range(KT):
                post_b(NCH - 1, at)


_INS = ["x_prompt", "x_sample", "state_conv", "state_hgrn", "norm_pre", "w_in", "conv_w", "hgrn_lb_logits",
        "hgrn_onorm", "w_out", "norm_post"]
_OUTS = [(1, NP, D), (NB, NS, D), (1, 1, 2, D), (1, NB, 2, D), (1, 1, KT, P, P), (1, NB, KT, P, P)]


def kernel(**inputs):
    import numpy as _np
    import concourse.bacc as _bacc
    from concourse.bass_utils import run_bass_kernel_spmd as _run

    nc = _bacc.Bacc("TRN2", target_bir_lowering=False, num_devices=1)
    arrays, args = {}, []
    for name in _INS:
        a = _np.ascontiguousarray(inputs[name])
        arrays[f"in_{name}"] = a
        args.append(nc.dram_tensor(f"in_{name}", a.shape, F32, kind="ExternalInput").ap())
    for i, shape in enumerate(_OUTS):
        args.append(nc.dram_tensor(f"out_{i}", shape, F32, kind="ExternalOutput").ap())
    build(nc, *args)
    r = _run(nc, [arrays], core_ids=[0])
    return tuple(r.results[0][f"out_{i}"] for i in range(len(_OUTS)))
```

```python
from contextlib import ExitStack

import concourse.bass as bass
from concourse import mybir

F32 = mybir.dt.float32
F32R = mybir.dt.float32r
U8 = mybir.dt.uint8
ALU = mybir.AluOpType
ACT = mybir.ActivationFunctionType
AX = mybir.AxisListType

P = 128
D = 1024
KT = D // P
NP = 1024
NB, NS = 8, 4
NSAMP = NB * NS
T = NP + NSAMP
CH = T // 3
NCH = 3
CK = NP // P
EPS = 1e-6
F_FLOOR = 2.061153622438558e-09
QSCALE = float(P) ** -0.5
B4 = 4
LEVELS = (4, 8, 16, 32, 64)
TT = CK + 1
HALF = D // 2
ORDER2 = (4, 0, 5, 1, 6, 2, 8, 3, 7)
PARTS = 4


class Events:

    def __init__(self, sem, names):
        self.sem, self.names = sem, list(names)
        self.index = {n: k for k, n in enumerate(self.names)}
        self.cursor = 0

    def now(self, name):
        assert self.names[self.cursor % len(self.names)] == name, (name, self.names[self.cursor % len(self.names)])
        self.cursor += 1
        return self.sem

    def at(self, round_, name):
        return round_ * len(self.names) + self.index[name] + 1


def build(nc, x_prompt, x_sample, state_conv, state_hgrn, norm_pre, w_in, conv_w, lb_logits, onorm,
          w_out, norm_post, y_prompt, y_sample, conv_p, conv_s, hgrn_p, hgrn_s):
    ctx = ExitStack()
    with ctx:
        def sb(name, shape, dt=F32):
            return ctx.enter_context(nc.sbuf_tensor(name, shape, dt))

        def sem(name):
            return ctx.enter_context(nc.semaphore(name))

        REG = 2 * KT * T
        reg_a = sb("reg_a", [P, REG], F32R)
        reg_b = sb("reg_b", [P, REG], F32R)
        wsplit = sb("wsplit", [P, 2, 2, KT, P], F32R)
        wraw = sb("wraw", [P, 2, KT, P])

        def halves(reg):
            return [reg[:, i * KT * T:(i + 1) * KT * T].rearrange("p (k t) -> p k t", k=KT) for i in range(2)]

        def wout_tile(reg, m):
            if m < 2:
                return [wsplit[:, m, i].rearrange("p k c -> p (k c)") for i in range(2)]
            at = 2 * (m - 2) * D
            return [reg[:, at + i * D:at + (i + 1) * D] for i in range(2)]

        ident = sb("ident", [P, P])
        cst = sb("cst", [P, 65])
        PRE, POST, CW, LBL, ONRM = 0, 2 * KT, 4 * KT, 7 * KT, 8 * KT
        lb = sb("lb", [P, 2, KT])
        eps = sb("eps", [P, 1])
        masks = {m: sb(f"mask{m}", [P, P // 2], U8) for m in LEVELS if m < 64}
        mask4 = sb("mask_within4", [P, P])
        bmask = sb("bmask", [P, NB])
        small = sb("small", [P, 48])

        ARENA = 11744
        arena = sb("arena", [P, ARENA])

        class Plan:
            def __init__(self, at=0):
                self.at = at

            def take(self, n):
                self.at += n
                assert self.at <= ARENA, self.at
                return arena[:, self.at - n:self.at]

        pl = Plan()
        st_x = [pl.take(D) for _ in range(3)]
        st_n = [pl.take(D) for _ in range(2)]
        st_t = [pl.take(D) for _ in range(2)]
        st_row = pl.take(D)
        st_vec = pl.take(P)
        st_scr = pl.take(D)
        st_lb = pl.take(4 * KT).rearrange("p (a k) -> p a k", a=4)
        c_st = pl.take(KT * 2 * NB)
        c_last = pl.take(KT * 18)
        st_ms = pl.take(6 * 64)
        c_last18 = st_row
        pl = Plan()
        UL = 2 + NP
        c_v = pl.take(T)
        c_u = pl.take(UL + NB * (NS + 2))
        c_acc = pl.take(T)
        c_g = pl.take(T)
        c_o = pl.take(T)
        c_w = pl.take(3)
        pl = Plan()
        r_am = pl.take(CK * P)
        r_kt = pl.take((CK + 1) * P)
        r_K = pl.take(T)
        r_Q, r_f, r_q, r_kr, r_vr, r_g = [pl.take(T) for _ in range(6)]
        r_vt = pl.take((CK + 1) * P)
        r_s = pl.take(CK * P)
        assert pl.at <= ARENA
        r_tt = sb("r_tt", [P, T // 2])
        r_qb = sb("r_qb", [P, NB * (NSAMP + NS)])
        r_os = sb("r_os", [P, P])
        r_as = sb("r_as", [NSAMP, NSAMP])
        lbh = sb("lbh", [P, 2])
        r_o = r_kr
        r_sq = r_Q
        def rows_at(at):
            return arena[:, at:at + D]

        o_x = [rows_at(i * D) for i in range(3)]
        o_n = [rows_at((3 + i) * D) for i in range(2)]
        o_t = rows_at(5 * D + 224 + T)
        o_g = rows_at(8 * T + 64)
        o_tr = [rows_at(8 * T + 64 + (1 + i) * D) for i in range(2)]
        assert 8 * T + 64 + 3 * D <= ARENA

        def o_part(i, half):
            rows = (wraw[:, 0].rearrange("p k c -> p (k c)"), wraw[:, 1].rearrange("p k c -> p (k c)"), r_q, r_vr)[i]
            return rows[:, half * HALF:(half + 1) * HALF]

        bank = [ctx.enter_context(nc.psum_tensor(f"bank{i}", [P, 512], F32)) for i in range(8)]
        x1_dram = nc.dram_tensor("x1_scratch", (T, D), F32, kind="Internal").ap()

        x_in = [sem(f"x_in{i}") for i in range(3)]
        vec_in, cst_in = sem("vec_in"), sem("cst_in")
        w_in_s = [sem(f"w_loaded{i}") for i in range(2)]
        w_hi, w_lo = sem("w_hi"), sem("w_lo")
        proj_done = sem("proj_done")
        bank_free = [sem(f"bank_free{i}") for i in range(3)]
        pool_ev = Events(sem("pool_ev"), ["id0", "id"] + [f"m{m}{s}" for m in LEVELS if m < 64 for s in "abc"]
                         + ["b0", "b1", "b2", "d0", "d1", "d2", "qb0"])
        S_AN = Events(sem("start_act_norm"), ["sq", "sd"])
        S_AT = Events(sem("start_act_split"), ["hi"])
        S_DN = Events(sem("start_dve_norm"), ["rs", "xn"])
        S_DT = Events(sem("start_dve_split"), ["ta", "tb", "lo"])
        S_PE = Events(sem("start_pe"), ["ta", "tb"])
        K_PE, K_DVE, K_ACT = sem("const_pe"), sem("const_dve"), sem("const_act")
        C_ACT = Events(sem("conv_act"), ["g0", "g1", "g2", "h0", "h1", "h2"])
        C_DVE = Events(sem("conv_dve"), ["st", "cw", "a0", "a1", "a2", "last", "o0", "o1", "o2", "l0", "l1", "l2"])
        tail_pe, tail_act = sem("state_pe"), sem("state_act")
        y_done, w_used, part_done, part_moved = sem("y_done"), sem("w_out_used"), sem("part_done"), sem("part_moved")
        A_PO = Events(sem("out_act"), ["s0", "s1", "sd1", "sq", "sd2"])
        V_PO = Events(sem("out_dve"), ["ms", "rs", "t0", "t1", "x1", "rs2", "xn"])
        P_TR = Events(sem("turn_pe"), ["ta", "tb"])
        V_TR = Events(sem("turn_dve"), ["ga", "gb", "lo"])
        A_TR = Events(sem("turn_act"), ["hi"])
        A_P2 = Events(sem("out2_act"), ["s0", "s1", "sd1"])
        V_P2 = Events(sem("out2_dve"), ["ms", "rs", "t0", "t1", "x"])
        V_Y = Events(sem("out2_sum"), ["y0", "y1"])
        q_sig, z_sig = sem("q_sig"), sem("z_sig")
        PR = Events(sem("rec_pe"), ["vt", "dg", "L4", "kst", "L8", "os", "L16", "us", "L32", "L64",
                                    "kt", "u", "o0", "o1"])
        VR = Events(sem("rec_dve"), ["lb", "qc", "k", "fa", "f", "tt", "rf", "rt", "q0", "q2", "q3", "k0", "k2", "k3",
                                     "vs", "am", "as", "w2", "u2", "qb", "w4", "c4", "u4", "w8", "c8", "u8", "w16", "c16", "u16", "w32", "c32", "u32", "ss",
                                     "sn0", "snew", "w64", "c64", "u64"]
                    + [f"s{c}" for c in range(CK)] + ["r0", "r1", "rs", "rss", "on0", "on1", "ons"])
        AR = Events(sem("rec_act"), ["vt", "kts", "os", "sqs", "kt", "sq0", "sq1", "sd", "sds"])
        pool_rec = sem("rec_pool")
        ot_done, o_rdy, o_hi, o_lo = sem("ot_done"), sem("o_rdy"), sem("o_hi"), sem("o_lo")
        s0_in, s0_out, sp_out = sem("s0_in"), sem("s0_out"), sem("sp_out")
        g_in = sem("norm_post_in")
        xr_in = [sem(f"residual_in{i}") for i in range(3)]
        stored = [sem(f"rows_stored{i}") for i in range(3)]
        cout = sem("conv_out")

        NW1, NW2, NW3 = 4 * KT, 5 * KT, 9 * KT
        G_IN2, G_OUT2 = 3 * NW1, 6 * NW1

        def wsrc(w, col):
            return w[:, bass.ds(col, P)].rearrange("(k p) c -> p k c", p=P)

        def emptied(n):
            return n + 1

        def bank_use(n):
            return n - KT

        MID = 6.5

        SPLIT_OUT = {3: (1, 2), 4: (3,), 5: (4,), 6: (5,), 7: (6,), 8: (7,)}

        def rows_of(i):
            return P if i < CK else NSAMP

        FIRST = ((0, 0), (0, 1), (1, 0), (1, 1), (0, 2), (1, 2), (2, 0), (2, 1), (2, 2))

        block = ctx.enter_context(nc.Block())

        @block.sync
        def _(sp):
            def load_w(n, src, slot, half, guard=True):
                if guard:
                    sp.wait_ge(w_lo, n - 1)
                sp.dma_start(wraw[:, slot], src).then_inc(w_in_s[slot], 16)

            for src, row, n in ((norm_pre, PRE, 2), (norm_post, POST, 2), (conv_w[0], CW, 3), (lb_logits, LBL, 1)):
                sp.dma_start(st_vec[row:row + n * KT, :], src.rearrange("l (k p) -> (l k) p", p=P)).then_inc(vec_in, 16)
            sp.dma_start(st_vec[ONRM:ONRM + 1, :], onorm).then_inc(vec_in, 16)
            sp.dma_start(st_row[0:2 * NB, :], state_conv[0].rearrange("b w c -> (b w) c")).then_inc(cst_in, 16)
            for i in range(9):
                r = P if i < 8 else NSAMP
                if i >= 3:
                    sp.wait_ge(S_DN.sem, S_DN.at(i - 3, "xn"))
                src = x_prompt[0, i * P:(i + 1) * P, :] if i < 8 else x_sample.rearrange("b s d -> (b s) d")
                sp.dma_start(st_x[i % 3][0:r, :], src).then_inc(x_in[i % 3], 16)
                if i == 2:
                    load_w(0, wsrc(w_in[0], 0), 0, 0, False)
                    load_w(1, wsrc(w_in[0], 2 * D), 1, 0, False)
            COL0 = (0, 2 * D, D, 3 * D)
            for t in (2, 3):
                load_w(t, wsrc(w_in[0], COL0[t]), t % 2, 1)
            with sp.Fori(1, KT) as j:
                for t in range(4):
                    load_w(j * 4 + t, wsrc(w_in[0], j * P + COL0[t]), t % 2, None)
            def wrows(w, k):
                return w[k * P:(k + 1) * P, :].rearrange("p (k c) -> p k c", k=KT)

            def x_rows(i, out):
                p, s = (y_prompt, y_sample) if out else (x_prompt, x_sample)
                return p[0, i * P:(i + 1) * P, :] if i < CK else s.rearrange("b s d -> (b s) d")

            def load_x(i):
                if i >= 3:
                    sp.wait_ge(V_PO.sem, V_PO.at(i - 3, "xn"))
                    sp.wait_ge(stored[i % 3], 16 * (i // 3))
                sp.dma_start(o_x[i % 3][0:rows_of(i), :], x_rows(i, False)).then_inc(xr_in[i % 3], 16)

            for k in range(KT):
                load_w(NW1 + k, wrows(w_out[0], k), k % 2, None)
            sp.wait_ge(tail_act, 2)
            sp.dma_start(conv_p[0, 0], c_last18[0:2, :]).then_inc(cout, 16)
            sp.dma_start(conv_s[0].rearrange("b w c -> (b w) c"), c_last18[2:18, :]).then_inc(cout, 16)
            sp.wait_ge(C_DVE.sem, C_DVE.at(KT - 1, "l2"))
            sp.wait_ge(C_ACT.sem, C_ACT.at(KT - 1, "h2"))
            sp.wait_ge(tail_pe, 2)
            sp.wait_ge(cout, 32)
            sp.dma_start(o_g, norm_post[0:1, :].broadcast_to([P, D])).then_inc(g_in, 16)
            QC, FC, VC, ZC = 0, D, 2 * D, 3 * D
            for i in range(TT):
                if i == 0:
                    for first in range(3):
                        load_x(first)
                    load_w(NW2, wsrc(w_in[1], QC), 0, None)
                    load_w(NW2 + 1, wsrc(w_in[1], VC), 1, None)
                sp.wait_ge(V_PO.sem, V_PO.at(i, "x1"))
                sp.dma_start(x1_dram[i * P:i * P + rows_of(i), :], o_x[i % 3][0:rows_of(i), :]).then_inc(stored[i % 3], 16)
                if i + 3 < TT:
                    load_x(i + 3)
            load_w(NW2 + 2, wsrc(w_in[1], FC), 0, None)
            with sp.Fori(1, KT) as j:
                for t, col in enumerate((QC, ZC - P, VC, FC)):
                    load_w(NW2 - 1 + t + j * 4, wsrc(w_in[1], j * P + col), (1 + t) % 2, None)
            load_w(NW3 - 1, wsrc(w_in[1], ZC + (KT - 1) * P), 1, None)
            for k in range(KT):
                load_w(NW3 + k, wrows(w_out[1], k), k % 2, None)
            for i in range(3):
                sp.wait_ge(stored[i], 48)
            sp.wait_ge(s0_out, KT * 16)
            sp.wait_ge(sp_out, KT * 16)
            sp.wait_ge(o_lo, KT)

            def load_x1(n):
                i = ORDER2[n]
                if n >= 3:
                    sp.wait_ge(stored[n % 3], 48 + 16 * (n // 3))
                sp.dma_start(o_x[n % 3][0:rows_of(i), :], x1_dram[i * P:i * P + rows_of(i), :]).then_inc(xr_in[n % 3], 16)

            load_x1(0)
            sp.dma_start(o_g, norm_post[1:2, :].broadcast_to([P, D])).then_inc(g_in, 16)
            load_x1(1)
            load_x1(2)
            for n in range(TT):
                i = ORDER2[n]
                sp.wait_ge(V_P2.sem, V_P2.at(n, "x"))
                sp.dma_start(x_rows(i, True), o_x[n % 3][0:rows_of(i), :]).then_inc(stored[n % 3], 16)
                if n + 3 < TT:
                    load_x1(n + 3)
            sp.wait_ge(cout, 32)
            for i in range(3):
                sp.wait_ge(stored[i], 96)

        @block.gpsimd
        def _(pool):
            pool.memset(ident[:, :], 0.0).then_inc(pool_ev.now("id0"), 1)
            pool.wait_ge(pool_ev.sem, pool_ev.at(0, "id0"))
            pool.affine_select(out=ident[:, :], in_=ident[:, :], compare_op=ALU.not_equal, fill=1.0, base=0,
                               pattern=[[-1, P]], channel_multiplier=1).then_inc(pool_ev.now("id"), 1)
            for i, m in enumerate(LEVELS[:-1]):
                scr = st_ms[:, 64 * i:64 * i + 64]
                v = scr.rearrange("p (b r) -> p b r", r=m)
                nb = 64 // m
                pool.memset(scr, 1.0).then_inc(pool_ev.now(f"m{m}a"), 1)
                pool.wait_ge(pool_ev.sem, pool_ev.at(0, f"m{m}a"))
                pool.affine_select(out=v, in_=v, compare_op=ALU.is_ge, fill=0.0, base=0,
                                   pattern=[[-2 * m, nb], [0, m]], channel_multiplier=1).then_inc(pool_ev.now(f"m{m}b"), 1)
                pool.wait_ge(pool_ev.sem, pool_ev.at(0, f"m{m}b"))
                pool.affine_select(out=v, in_=v, compare_op=ALU.is_ge, fill=0.0, base=m - 1,
                                   pattern=[[2 * m, nb], [0, m]], channel_multiplier=-1).then_inc(pool_ev.now(f"m{m}c"), 1)
            pool.memset(bmask[:, :], 1.0).then_inc(pool_ev.now("b0"), 1)
            pool.wait_ge(pool_ev.sem, pool_ev.at(0, "b0"))
            pool.affine_select(out=bmask[:, :], in_=bmask[:, :], compare_op=ALU.is_ge, fill=0.0, base=0,
                               pattern=[[-NS, NB]], channel_multiplier=1).then_inc(pool_ev.now("b1"), 1)
            pool.wait_ge(pool_ev.sem, pool_ev.at(0, "b1"))
            pool.affine_select(out=bmask[:, :], in_=bmask[:, :], compare_op=ALU.is_ge, fill=0.0, base=NS - 1,
                               pattern=[[NS, NB]], channel_multiplier=-1).then_inc(pool_ev.now("b2"), 1)
            pool.memset(mask4[:, :], 1.0).then_inc(pool_ev.now("d0"), 1)
            pool.wait_ge(pool_ev.sem, pool_ev.at(0, "d0"))
            v = mask4[:, :].rearrange("p (b r) -> p b r", r=B4)
            pool.affine_select(out=v, in_=v, compare_op=ALU.is_ge, fill=0.0, base=0,
                               pattern=[[-B4, P // B4], [0, B4]], channel_multiplier=1).then_inc(pool_ev.now("d1"), 1)
            pool.wait_ge(pool_ev.sem, pool_ev.at(0, "d1"))
            pool.affine_select(out=v, in_=v, compare_op=ALU.is_ge, fill=0.0, base=0,
                               pattern=[[B4, P // B4], [1, B4]], channel_multiplier=-1).then_inc(pool_ev.now("d2"), 1)
            pool.memset(r_qb[:, :], 0.0).then_inc(pool_ev.now("qb0"), 1)

            def spread_v(h):
                pool.wait_ge(VR.sem, VR.at(h, "vs"))
                pool.tensor_tensor(r_kt[0:NSAMP, 0:NB * P].rearrange("p (b v) -> p b v", b=NB),
                                   r_vt[0:NSAMP, CK * P:].unsqueeze(1).broadcast_to([NSAMP, NB, P]),
                                   bmask[0:NSAMP, :].unsqueeze(2).broadcast_to([NSAMP, NB, P]),
                                   ALU.mult).then_inc(pool_rec, 1)

            spread_v(0)
            with pool.Fori(1, KT) as h:
                spread_v(h)

        @block.tensor
        def _(pe):
            pe.wait_ge(pool_ev.sem, pool_ev.at(0, "id"))
            pe.wait_ge(vec_in, 5 * 16)
            nc.tensor.transpose(bank[7][:, 0:65], st_vec[0:65, :], ident[0:65, 0:65]).then_inc(K_PE, 1)
            pe.wait_ge(cst_in, 16)
            for k in range(KT):
                mm = nc.tensor.transpose(bank[6][:, k * 16:(k + 1) * 16], st_row[0:16, k * P:(k + 1) * P],
                                         ident[0:16, 0:16])
                if k < NCH:
                    mm.then_inc(bank_free[k], 1)
            mm.then_inc(K_PE, 1)
            pe.wait_ge(K_DVE, 2)
            pairs = ((3, 4), (5, 6))
            for i in range(9):
                r = P if i < 8 else NSAMP
                pe.wait_ge(S_DN.sem, S_DN.at(i, "xn"))
                if i >= 2:
                    pe.wait_ge(S_DT.sem, S_DT.at(i - 2, "tb"))
                for half in range(2):
                    for k in range(4):
                        kk = half * 4 + k
                        mm = nc.tensor.transpose(bank[pairs[i % 2][half]][:, k * P:k * P + r],
                                                 st_n[i % 2][0:r, kk * P:(kk + 1) * P], ident[0:r, 0:r])
                    mm.then_inc(S_PE.now("ta" if half == 0 else "tb"), 1)

            def group(b, w, src, c, use, mid=None):
                pe.wait_ge(bank_free[b], emptied(use))
                for k in range(KT):
                    if mid and k == KT // 2:
                        mid()
                    rhs = [s[:, k, c * CH:(c + 1) * CH] for s in src]
                    for i, (wi, hi) in enumerate(((0, 0), (1, 0), (0, 1))):
                        mm = nc.tensor.matmul(bank[b][:, 0:CH], w[wi][:, k, :], rhs[hi],
                                              start=(k == 0 and i == 0), stop=(k == KT - 1 and i == 2))
                mm.then_inc(proj_done, 1)

            def slot(i):
                return [wsplit[:, i, 0], wsplit[:, i, 1]]

            h0, o0 = halves(reg_a), halves(reg_b)
            with pe.Fori(0, KT) as j:
                for t in range(4):
                    pe.wait_ge(w_lo, j * 4 + t + 1)
                    for c in range(NCH):
                        if t == 0:
                            pe.wait_ge(S_DT.sem, S_DT.at((2, 5, 8)[c], "lo"))
                        group(c, slot(t % 2), h0, c, j * 4 + t)
            pe.wait_ge(C_DVE.sem, C_DVE.at(KT - 1, "last"))
            for half in range(2):
                for k in range(4):
                    kk = half * 4 + k
                    mm = nc.tensor.transpose(bank[6 + half][0:18, k * P:(k + 1) * P],
                                             c_last[:, kk * 18:(kk + 1) * 18], ident[:, :])
                mm.then_inc(tail_pe, 1)

            def products(k, halves_, w, src, i, start, stop):
                r = rows_of(i)
                for side, terms in ((0, (0, 1)), (1, (0,))):
                    for b, half in halves_:
                        for wi in terms:
                            mm = nc.tensor.matmul(bank[b][0:r, :], src[side][:, k, i * P:i * P + r],
                                                  w[wi][:, half * HALF:(half + 1) * HALF],
                                                  start=(start and side == 0 and wi == 0), stop=(stop and side == 1))
                return mm

            def turn_rows(i):
                r = rows_of(i)
                pe.wait_ge(V_PO.sem, V_PO.at(i, "xn"))
                if i:
                    pe.wait_ge(V_TR.sem, V_TR.at(i - 1, "gb"))
                for half, name in enumerate(("ta", "tb")):
                    for k in range(4):
                        kk = half * 4 + k
                        mm = nc.tensor.transpose(bank[6 + half][:, k * P:k * P + r],
                                                 o_n[i % 2][0:r, kk * P:(kk + 1) * P], ident[0:r, 0:r])
                    mm.then_inc(P_TR.now(name), 1)

            for k in range(KT):
                pe.wait_ge(w_lo, NW1 + k + 1)
                pe.wait_ge(C_DVE.sem, C_DVE.at(k, "l2"))
                if k == 0:
                    for b in range(NCH):
                        pe.wait_ge(bank_free[b], emptied(NW1))
                    pe.wait_ge(tail_act, 2)
                for i in range(3):
                    mm = products(k, ((2 * i, 0), (2 * i + 1, 1)), wout_tile(reg_a, k), o0, i, k == 0, k == KT - 1)
                    if k == KT - 1:
                        mm.then_inc(y_done, 1)
            TURN = {(3, 3): 0, (4, 3): 1, (4, 7): 2, (5, 7): 3, (6, 3): 4, (6, 7): 5, (7, 7): 6, (8, 7): 7}
            for i in range(3, TT):
                pe.wait_ge(V_PO.sem, V_PO.at(i - 3, "t1"))
                for k in range(KT):
                    b = 2 * (i % 3)
                    mm = products(k, ((b, 0), (b + 1, 1)), wout_tile(reg_a, k), o0, i, k == 0, k == KT - 1)
                    if k == KT - 1:
                        mm.then_inc(y_done, 1)
                    elif i == TT - 1 and k < 2:
                        mm.then_inc(w_used, 1)
                    if (i, k) in TURN:
                        turn_rows(TURN[i, k])

            h1, o1 = halves(reg_b), halves(reg_a)

            def tokens(c, n=P):
                return slice(c * P, c * P + n)

            def level(h, m):
                b = bank[3 + LEVELS.index(m) % 2]
                if m == 64:
                    for c in range(CK):
                        mm = nc.tensor.matmul(b[0:64, c * 64:(c + 1) * 64], r_K[:, tokens(c, 64)],
                                              r_Q[:, c * P + 64:(c + 1) * P], start=True, stop=True)
                else:
                    for c in range(CK):
                        rhs = r_Q[:, tokens(c)].rearrange("p (b two r) -> p b two r", two=2, r=m)[:, :, 1, :]
                        mm = nc.tensor.matmul(b[:, c * 64:(c + 1) * 64].rearrange("p (b r) -> p b r", r=m),
                                              r_K[:, tokens(c)], rhs, start=True, stop=True)
                mm.then_inc(PR.now(f"L{m}"), 1)

            def turn_output(h):
                pe.wait_ge(VR.sem, VR.at(h, "ons"))
                for c in range(CK):
                    nc.tensor.transpose(bank[5 + c // 4][:, tokens(c % 4)], r_kt[:, tokens(c)], ident[:, :])
                nc.tensor.transpose(bank[7][:, 256:256 + NSAMP], r_kt[0:NSAMP, CK * P:],
                                    ident[0:NSAMP, 0:NSAMP]).then_inc(ot_done, 1)

            def rec(h, s, last):
                if s == 0:
                    if last is not None:
                        turn_output(last)
                elif s == 1:
                    for c in range(NCH):
                        pe.wait_ge(bank_free[c], emptied(bank_use(NW2) + 2 + 4 * h))
                    if last is not None:
                        pe.wait_ge(o_rdy, last + 1)
                    for c in range(CK):
                        nc.tensor.transpose(bank[5 + c // 4][:, tokens(c % 4)], r_vr[:, tokens(c)], ident[:, :])
                    nc.tensor.transpose(bank[7][0:NSAMP, 128:256], r_vr[:, NP:], ident[:, :]).then_inc(PR.now("vt"), 1)
                elif s == 3:
                    pe.wait_ge(VR.sem, VR.at(h, "vs"))
                    for c in range(CK):
                        nc.tensor.matmul(bank[3 + c // 4][:, tokens(c % 4)], r_K[:, tokens(c)], r_Q[:, tokens(c)],
                                         start=True, stop=True)
                    nc.tensor.matmul(bank[7][0:NSAMP, 0:NSAMP], r_K[:, NP:], r_Q[:, NP:], start=True,
                                     stop=True).then_inc(PR.now("dg"), 1)
                elif s == 4:
                    pe.wait_ge(VR.sem, VR.at(h, "w2"))
                    level(h, 4)
                    nc.tensor.transpose(bank[7][0:NSAMP, 0:P], r_K[:, NP:], ident[:, :]).then_inc(PR.now("kst"), 1)
                elif s == 5:
                    pe.wait_ge(AR.sem, AR.at(h, "kts"))
                    pe.wait_ge(s0_in, h * 16 + 16)
                    pe.wait_ge(VR.sem, VR.at(h, "w4"))
                    level(h, 8)
                    nc.tensor.matmul(bank[7][0:NSAMP, 0:P], r_as[0:NSAMP, :], r_vt[0:NSAMP, CK * P:],
                                     start=True, stop=False)
                    for b in range(NB):
                        mm = nc.tensor.matmul(bank[7][0:NSAMP, 0:P], r_qb[:, b * NSAMP:(b + 1) * NSAMP], r_s[:, tokens(b)],
                                              start=False, stop=(b == NB - 1))
                    mm.then_inc(PR.now("os"), 1)
                elif s == 6:
                    pe.wait_ge(VR.sem, VR.at(h, "w8"))
                    level(h, 16)
                    pe.wait_ge(pool_rec, h + 1)
                    pe.wait_ge(AR.sem, AR.at(h, "vt"))
                    for half in range(2):
                        mm = nc.tensor.matmul(bank[5 + half][:, :], r_kt[0:NSAMP, CK * P:],
                                              r_kt[0:NSAMP, half * 512:(half + 1) * 512], start=True, stop=True)
                    mm.then_inc(PR.now("us"), 1)
                elif s == MID:
                    pe.wait_ge(VR.sem, VR.at(h, "w16"))
                    level(h, 32)
                elif s == 7:
                    pe.wait_ge(VR.sem, VR.at(h, "w32"))
                    level(h, 64)
                elif s == 8:
                    pe.wait_ge(VR.sem, VR.at(h, "w64"))
                    for c in range(CK):
                        mm = nc.tensor.transpose(bank[5 + c // 4][:, tokens(c % 4)], r_K[:, tokens(c)], ident[:, :])
                    mm.then_inc(PR.now("kt"), 1)
                elif s == 9:
                    pe.wait_ge(AR.sem, AR.at(h, "kt"))
                    for c in range(CK):
                        mm = nc.tensor.matmul(bank[5 + c // 4][:, tokens(c % 4)], r_kt[:, tokens(c)], r_vt[:, tokens(c)],
                                              start=True, stop=True)
                    mm.then_inc(PR.now("u"), 1)
                elif s == 10:
                    pe.wait_ge(VR.sem, VR.at(h, f"s{CK - 1}"))
                    for c in range(CK):
                        dst = bank[3 + c // 4][:, tokens(c % 4)]
                        mm = nc.tensor.matmul(dst, r_am[:, tokens(c)], r_vt[:, tokens(c)], start=True, stop=(c == 0))
                        if c:
                            mm = nc.tensor.matmul(dst, r_Q[:, tokens(c)], r_s[:, tokens(c - 1)], start=False, stop=True)
                        if c % 4 == 3:
                            mm.then_inc(PR.now(f"o{c // 4}"), 1)

            def tile(n, s, use):
                pe.wait_ge(w_lo, n + 1)
                for c in range(NCH):
                    yield lambda c=c, mid=None: group(c, slot(s), h1, c, use, mid)

            for n, (i, c) in enumerate(FIRST):
                pe.wait_ge(w_lo, NW2 + i + 1)
                if i == 0:
                    pe.wait_ge(V_TR.sem, V_TR.at((2, 5, 8)[c], "lo"))
                    pe.wait_ge(V_PO.sem, V_PO.at((6, 6, 7)[c], "t1"))
                group(c, slot(i % 2), h1, c, bank_use(NW2 + i))
                if n == 1:
                    turn_rows(TT - 1)

            def iteration(j, last):
                base = NW2 - 1 + 4 * j
                for t in range(4):
                    runs = list(tile(base + t, (1 + t) % 2, bank_use(base + t)))
                    for c in range(NCH):
                        runs[c](mid=(lambda: rec(j - 1, MID, last)) if 3 * t + c == 7 else None)
                        rec(j - 1, 3 * t + c, last)

            iteration(1, None)
            with pe.Fori(2, KT) as j:
                iteration(j, j - 2)

            def part(n, ks):
                if ks[0] == 0:
                    if n >= NCH:
                        pe.wait_ge(part_moved, n - 2)
                    else:
                        pe.wait_ge(bank_free[n], emptied(bank_use(NW3)))
                for k in ks:
                    mm = products(k, ((n % 3, n % 2),), wout_tile(reg_b, k), o1, n // 2, k == 0, k == KT - 2)
                if ks[-1] == KT - 2:
                    mm.then_inc(part_done, 1)

            def first_parts(*ks):
                for k in ks:
                    pe.wait_ge(w_lo, NW3 + k + 1)
                    if k == 0:
                        pe.wait_ge(o_lo, KT - 1)
                    for n in range(NCH):
                        part(n, (k,))

            others = tuple(range(KT - 1))
            FILL = {4: (0, 1), 5: (2,), 6: (3,), 7: (4,), 8: (5, 6)}
            FILL2 = {9: (3,), 10: (4, 5), 11: (6, 7)}
            runs = list(tile(NW3 - 1, 1, bank_use(NW3 - 1)))
            for s in range(12):
                if s < NCH:
                    runs[s]()
                if s == 7:
                    rec(KT - 1, MID, KT - 2)
                rec(KT - 1, s, KT - 2)
                first_parts(*FILL.get(s, ()))
                for n in FILL2.get(s, ()):
                    part(n, others)
            pe.wait_ge(part_moved, 2 * PARTS - 1)
            turn_output(KT - 1)
            pe.wait_ge(part_moved, 2 * PARTS)
            for n, i in enumerate(ORDER2):
                b = 2 * (n % 4)
                where = ((b, 0), (b + 1, 1))
                if n >= 4:
                    pe.wait_ge(V_P2.sem, V_P2.at(n - 4, "t1"))
                elif n == 1:
                    pe.wait_ge(o_rdy, KT)
                if i >= PARTS:
                    for k in range(KT - 1):
                        products(k, where, wout_tile(reg_b, k), o1, i, k == 0, False)
                if n == 0:
                    pe.wait_ge(o_lo, KT)
                    pe.wait_ge(w_lo, NW3 + KT)
                products(KT - 1, where, wout_tile(reg_b, KT - 1), o1, i, i < PARTS, True).then_inc(y_done, 1)

        @block.scalar
        def _(act):
            A = nc.scalar.activation

            def split_hi(s, half, used, dst=None):
                act.wait_ge(w_in_s[s], half * 16)
                act.wait_ge(proj_done, used)
                A(wsplit[:, s, 0] if dst is None else dst, wraw[:, s], ACT.Copy).then_inc(w_hi, 1)

            act.wait_ge(K_DVE, 3)
            A(st_lb[:, 1], st_lb[:, 0], ACT.Exp).then_inc(K_ACT, 1)

            def normalise(i):
                r = P if i < 8 else NSAMP
                act.wait_ge(x_in[i % 3], 16 * (i // 3 + 1))
                if i:
                    act.wait_ge(S_AN.sem, S_AN.at(i - 1, "sq"))
                A(st_scr[0:r, :], st_x[i % 3][0:r, :], ACT.Square,
                  accum_out=small[0:r, i:i + 1]).then_inc(S_AN.now("sq"), 1)
                act.wait_ge(S_AN.sem, S_AN.at(i, "sq"))
                A(small[0:r, 16 + i:17 + i], small[0:r, i:i + 1], ACT.Sqrt, bias=eps[0:r, :],
                  scale=1.0 / D).then_inc(S_AN.now("sd"), 1)

            normalise(0)
            for i in range(9):
                r = P if i < 8 else NSAMP
                if i < 8:
                    normalise(i + 1)
                act.wait_ge(S_DT.sem, S_DT.at(i, "tb"))
                A(halves(reg_a)[0][:, :, i * P:i * P + r], st_t[i % 2].rearrange("p (k t) -> p k t", k=KT)[:, :, 0:r],
                  ACT.Copy).then_inc(S_AT.now("hi"), 1)
                if i == 2:
                    split_hi(0, 1, 0)
            act.wait_ge(S_DT.sem, S_DT.at(8, "lo"))

            with act.Fori(0, KT) as j:
                for t in range(4):
                    n3 = 12 * j + 3 * t
                    split_hi((t + 1) % 2, j * 2 + ((t + 1) // 2 + 1), n3 + 1)
                    if t == 0:
                        for c in range(NCH):
                            act.wait_ge(proj_done, n3 + (c + 1))
                            A(c_v[:, c * CH:(c + 1) * CH], bank[c][:, 0:CH], ACT.Copy).then_inc(bank_free[c], 1)
                    if t == 3:
                        for c in range(NCH):
                            act.wait_ge(proj_done, n3 + (c + 1))
                            A(c_g[:, c * CH:(c + 1) * CH], bank[c][:, 0:CH], ACT.Sigmoid).then_inc(C_ACT.now(f"g{c}"), 1)
                        for c in range(NCH):
                            act.wait_ge(C_DVE.sem, C_DVE.at(j, f"o{c}"))
                            A(reg_b[:, bass.ds(j * T + c * CH, CH)], c_o[:, c * CH:(c + 1) * CH],
                              ACT.Copy).then_inc(C_ACT.now(f"h{c}"), 1)
            for half in range(2):
                act.wait_ge(tail_pe, 2)
                A(c_last18[0:18, half * 512:(half + 1) * 512], bank[6 + half][0:18, :], ACT.Copy).then_inc(tail_act, 1)

            def square(src, dst, ev, name, col, r):
                A(dst[0:r, :], src, ACT.Square, accum_out=small[0:r, col:col + 1]).then_inc(ev.now(name), 1)

            def col(n, what):
                return 8 * (n % 2) + ("a", "b", "ms", "sd", "rs", "ms2", "sd2", "rs2").index(what)

            def root(n, src, dst, r, scale=1.0 / D):
                return A(small[0:r, col(n, dst):col(n, dst) + 1], small[0:r, col(n, src):col(n, src) + 1], ACT.Sqrt,
                         bias=eps[0:r, :], scale=scale)

            def squares_y(i):
                r = rows_of(i)
                if i >= 2:
                    act.wait_ge(P_TR.sem, P_TR.at(i - 2, "tb"))
                act.wait_ge(y_done, i + 1)
                for half in range(2):
                    square(bank[2 * (i % 3) + half][0:r, :], o_n[i % 2][:, half * HALF:(half + 1) * HALF], A_PO,
                           f"s{half}", col(i, "ab"[half]), r)

            def turned_hi(i):
                r = rows_of(i)
                act.wait_ge(V_TR.sem, V_TR.at(i, "gb"))
                A(halves(reg_b)[0][:, :, i * P:i * P + r], o_tr[i % 2].rearrange("p (k t) -> p k t", k=KT)[:, :, 0:r],
                  ACT.Copy).then_inc(A_TR.now("hi"), 1)

            act.wait_ge(C_DVE.sem, C_DVE.at(KT - 1, "l2"))
            for k in range(1, KT):
                n = NW1 + k
                split_hi(n % 2, n // 2 + 1, G_IN2, wout_tile(reg_a, k)[0].rearrange("p (k c) -> p k c", k=KT))
            act.wait_ge(cout, 32)
            squares_y(0)
            for i in range(TT):
                r = rows_of(i)
                act.wait_ge(V_PO.sem, V_PO.at(i, "ms"))
                root(i, "ms", "sd", r).then_inc(A_PO.now("sd1"), 1)
                act.wait_ge(V_PO.sem, V_PO.at(i, "x1"))
                square(o_x[i % 3][0:r, :], o_n[i % 2], A_PO, "sq", col(i, "ms2"), r)
                act.wait_ge(A_PO.sem, A_PO.at(i, "sq"))
                root(i, "ms2", "sd2", r).then_inc(A_PO.now("sd2"), 1)
                if i:
                    turned_hi(i - 1)
                if i == TT - 2:
                    for m in range(2):
                        act.wait_ge(w_used, m + 1)
                        split_hi(m, (NW2 + m) // 2 + 1, G_IN2)
                if i + 1 < TT:
                    squares_y(i + 1)
            turned_hi(TT - 1)

            def turn_hi(h):
                act.wait_ge(o_rdy, h + 1)
                A(reg_a[:, bass.ds(h * T, T)], r_o, ACT.Copy).then_inc(o_hi, 1)

            states = r_s.rearrange("p (b v) -> p b v", b=NB)

            def rec(h, s, last):
                if s == 1:
                    if last is None:
                        act.wait_ge(V_TR.sem, V_TR.at(TT - 1, "lo"))
                    else:
                        act.wait_ge(sp_out, h * 16)
                    act.dma_start(states, state_hgrn[0, :, bass.ds(h, 1)].rearrange("b h k v -> k (b h) v")).then_inc(s0_in, 16)
                    act.wait_ge(PR.sem, PR.at(h, "vt"))
                    for half in range(2):
                        ins = A(r_vt[:, half * 512:(half + 1) * 512], bank[5 + half][:, :], ACT.Copy)
                    ins.then_inc(AR.now("vt"), 1)
                    if last is not None:
                        turn_hi(last)
                elif s == 4:
                    act.wait_ge(PR.sem, PR.at(h, "kst"))
                    A(r_kt[0:NSAMP, CK * P:], bank[7][0:NSAMP, 0:P], ACT.Copy).then_inc(AR.now("kts"), 1)
                elif s == 5:
                    act.wait_ge(PR.sem, PR.at(h, "os"))
                    A(r_os[0:NSAMP, :], bank[7][0:NSAMP, 0:P], ACT.Copy).then_inc(AR.now("os"), 1)
                    act.wait_ge(AR.sem, AR.at(h, "os"))
                    A(bank[7][0:NSAMP, P:2 * P], r_os[0:NSAMP, :], ACT.Square,
                      accum_out=small[0:NSAMP, CK:CK + 1]).then_inc(AR.now("sqs"), 1)
                elif s == 7:
                    act.wait_ge(VR.sem, VR.at(h, "snew"))
                    act.dma_start(hgrn_s[0, :, bass.ds(h, 1)].rearrange("b h k v -> k (b h) v"), states).then_inc(s0_out, 16)
                elif s == 8:
                    act.wait_ge(PR.sem, PR.at(h, "kt"))
                    for half in range(2):
                        ins = A(r_kt[:, half * 512:(half + 1) * 512], bank[5 + half][:, :], ACT.Copy)
                    ins.then_inc(AR.now("kt"), 1)
                elif s == 10:
                    act.wait_ge(PR.sem, PR.at(h, "o1"))
                    for half in range(2):
                        A(r_sq[:, half * 512:(half + 1) * 512], bank[3 + half][:, :], ACT.Square).then_inc(AR.now(f"sq{half}"), 1)
                    act.wait_ge(VR.sem, VR.at(h, "r1"))
                    A(small[:, 16:16 + CK], small[:, 0:CK], ACT.Sqrt, bias=eps[:, :], scale=1.0 / P).then_inc(AR.now("sd"), 1)
                    A(small[0:NSAMP, 16 + CK:17 + CK], small[0:NSAMP, CK:CK + 1], ACT.Sqrt, bias=eps[0:NSAMP, :],
                      scale=1.0 / P).then_inc(AR.now("sds"), 1)
                    act.wait_ge(VR.sem, VR.at(h, f"s{CK - 1}"))
                    act.dma_start(hgrn_p[0, 0, bass.ds(h, 1)].rearrange("h k v -> k (h v)"),
                                  r_s[:, (CK - 1) * P:]).then_inc(sp_out, 16)

            def evac(kind, c, done, h):
                act.wait_ge(proj_done, done)
                src = bank[c][:, 0:CH]
                cols = slice(c * CH, (c + 1) * CH)
                if kind == "q":
                    if h is not None and c == 0:
                        act.wait_ge(VR.sem, VR.at(h, "qc"))
                    A(r_q[:, cols], src, ACT.Sigmoid).then_inc(q_sig, 1)
                elif kind == "z":
                    A(r_g[:, cols], src, ACT.Sigmoid).then_inc(z_sig, 1)
                elif kind == "v":
                    A(r_vr[:, cols], src, ACT.Copy).then_inc(bank_free[c], 1)
                else:
                    A(r_f[:, cols], src, ACT.Sigmoid)
                    A(r_kr[:, cols], src, ACT.Sigmoid, scale=-1.0).then_inc(bank_free[c], 1)

            for n, (i, c) in enumerate(FIRST):
                if n == 6:
                    for k in range(3):
                        act.wait_ge(stored[k], 48)
                    act.wait_ge(V_TR.sem, V_TR.at(TT - 1, "lo"))
                evac("qvf"[i], c, G_IN2 + n + 1, None)
                if n == 4:
                    split_hi(0, (NW2 + 2) // 2 + 1, G_IN2 + 5)
                if n == 5:
                    split_hi(1, (NW2 + 3) // 2 + 1, G_IN2 + 6)

            def iteration(j, last):
                for t, kind in enumerate("qzvf"):
                    for c in range(NCH):
                        if c == 0:
                            split_hi(t % 2, 2 * j + (NW2 + t) // 2 + 1, G_IN2 - 3 + 3 * t + 12 * j)
                        evac(kind, c, G_IN2 - 3 + 3 * t + c + 1 + 12 * j, j - 1)
                        rec(j - 1, 3 * t + c, last)

            iteration(1, None)
            with act.Fori(2, KT) as j:
                iteration(j, j - 2)
            def move_parts(first, last):
                for n in range(first, last):
                    act.wait_ge(part_done, n + 1)
                    A(o_part(n // 2, n % 2), bank[n % 3][:, :], ACT.Copy).then_inc(part_moved, 1)

            def split_out(k):
                split_hi(k % 2, (NW3 + k) // 2 + 1, G_OUT2, wout_tile(reg_b, k)[0].rearrange("p (k c) -> p k c", k=KT))

            split_hi(0, NW3 // 2 + 1, G_OUT2 - 3)
            for s in range(12):
                if 2 <= s < 5:
                    evac("z", s - 2, G_OUT2 - 3 + s - 1, None)
                rec(KT - 1, s, KT - 2)
                for k in SPLIT_OUT.get(s, ()):
                    split_out(k)
                if s == 9:
                    act.wait_ge(w_lo, NW3 + KT)
                    move_parts(0, 3)
                if s == 10:
                    move_parts(3, 4)
            move_parts(4, 2 * PARTS)
            turn_hi(KT - 1)
            act.wait_ge(o_lo, KT)

            def squares_2(n):
                i = ORDER2[n]
                r = rows_of(i)
                if n >= 2:
                    act.wait_ge(V_P2.sem, V_P2.at(n - 2, "ms"))
                    act.wait_ge(A_P2.sem, A_P2.at(n - 2, "s1"))
                act.wait_ge(y_done, TT + n + 1)
                for half in range(2):
                    if i < PARTS:
                        act.wait_ge(V_Y.sem, V_Y.at(i, f"y{half}"))
                    src = o_part(i, half) if i < PARTS else bank[2 * (n % 4) + half]
                    square(src[0:r, :], o_n[n % 2][:, half * HALF:(half + 1) * HALF], A_P2,
                           f"s{half}", col(n, "ab"[half]), r)

            for n in range(TT):
                r = rows_of(ORDER2[n])
                squares_2(n)
                act.wait_ge(V_P2.sem, V_P2.at(n, "ms"))
                root(n, "ms", "sd", r).then_inc(A_P2.now("sd1"), 1)

        @block.vector
        def _(dve):
            V = nc.vector

            def split_lo(count, s, dst=None, hi=None):
                dve.wait_ge(w_hi, count)
                d, h = (wsplit[:, s, 1], wsplit[:, s, 0]) if dst is None else (dst, hi)
                V.tensor_tensor(d, wraw[:, s], h.bitcast(F32), ALU.subtract).then_inc(w_lo, 1)

            V.memset(eps[:, :], EPS)
            dve.wait_ge(K_PE, 1)
            V.tensor_copy(cst[:, :], bank[7][:, 0:65]).then_inc(K_DVE, 1)
            dve.wait_ge(K_PE, 2)
            V.tensor_copy(c_st, bank[6][:, 0:KT * 16]).then_inc(K_DVE, 1)
            dve.wait_ge(K_DVE, 2)
            V.tensor_tensor(st_lb[:, 0], cst[:, LBL:LBL + KT], cst[:, LBL:LBL + KT], ALU.subtract).then_inc(K_DVE, 1)
            dve.wait_ge(K_ACT, 1)
            V.reciprocal(st_lb[:, 2], st_lb[:, 1]).then_inc(K_DVE, 1)
            dve.wait_ge(K_DVE, 4)
            V.tensor_tensor(st_lb[:, 3], st_lb[:, 1], st_lb[:, 2], ALU.mult).then_inc(K_DVE, 1)
            dve.wait_ge(K_DVE, 5)
            V.tensor_tensor(lb[:, 0], st_lb[:, 3], st_lb[:, 3], ALU.subtract).then_inc(K_DVE, 1)
            dve.wait_ge(K_DVE, 6)
            V.tensor_scalar(lb[:, 1], lb[:, 0], -1.0, 1.0, ALU.mult, ALU.add).then_inc(K_DVE, 1)

            def normalise(i):
                r = P if i < 8 else NSAMP
                dve.wait_ge(S_AN.sem, S_AN.at(i, "sd"))
                V.reciprocal(small[0:r, 32 + i:33 + i], small[0:r, 16 + i:17 + i]).then_inc(S_DN.now("rs"), 1)
                dve.wait_ge(S_DN.sem, S_DN.at(i, "rs"))
                if i >= 2:
                    dve.wait_ge(S_PE.sem, S_PE.at(i - 2, "tb"))
                V.tensor_scalar(st_n[i % 2][0:r, :], st_x[i % 3][0:r, :], small[0:r, 32 + i:33 + i], None,
                                ALU.mult).then_inc(S_DN.now("xn"), 1)

            normalise(0)
            h_hi, h_lo = halves(reg_a)
            for i in range(9):
                r = P if i < 8 else NSAMP
                if i < 8:
                    normalise(i + 1)
                dst = st_t[i % 2].rearrange("p (k t) -> p k t", k=KT)
                if i >= 2:
                    dve.wait_ge(S_AT.sem, S_AT.at(i - 2, "hi"))
                for half, name in enumerate(("ta", "tb")):
                    dve.wait_ge(S_PE.sem, S_PE.at(i, name))
                    src = bank[((3, 4), (5, 6))[i % 2][half]][:, :].rearrange("p (k t) -> p k t", k=4)[:, :, 0:r]
                    g = cst[:, PRE + 4 * half:PRE + 4 * half + 4].unsqueeze(2).broadcast_to([P, 4, r])
                    V.tensor_tensor(dst[:, 4 * half:4 * half + 4, 0:r], src, g, ALU.mult).then_inc(S_DT.now(name), 1)
                dve.wait_ge(S_AT.sem, S_AT.at(i, "hi"))
                V.tensor_tensor(h_lo[:, :, i * P:i * P + r], dst[:, :, 0:r],
                                h_hi[:, :, i * P:i * P + r].bitcast(F32), ALU.subtract).then_inc(S_DT.now("lo"), 1)
                if i == 2:
                    split_lo(1, 0)
            dve.wait_ge(pool_ev.sem, pool_ev.at(0, "qb0"))
            for i, m in enumerate(LEVELS[:-1]):
                V.tensor_copy(masks[m][:, :], st_ms[:, 64 * i:64 * i + 64])

            V.memset(c_u[:, 0:2], 0.0)
            us = c_u[:, UL:].rearrange("p (b s) -> p b s", b=NB)
            accs = c_acc[:, NP:].rearrange("p (b s) -> p b s", b=NB)
            with dve.Fori(0, KT) as j:
                for t in range(4):
                    n3 = 12 * j + 3 * t
                    split_lo(4 * j + (t + 2), (t + 1) % 2)
                    if t == 0:
                        V.tensor_copy(us[:, :, 0:2], c_st[:, bass.ds(j * 2 * NB, 2 * NB)]
                                      .rearrange("p (b w) -> p b w", b=NB)).then_inc(C_DVE.now("st"), 1)
                        for w in range(3):
                            ins = V.tensor_copy(c_w[:, w:w + 1], cst[:, bass.ds(j + CW + w * KT, 1)])
                        ins.then_inc(C_DVE.now("cw"), 1)
                    if t == 1:
                        for c in range(NCH):
                            dve.wait_ge(proj_done, n3 + (c + 1))
                            dve.wait_ge(bank_free[c], emptied(4 * j + 1))
                            a, b = c * CH, min((c + 1) * CH, NP)
                            ins = V.tensor_tensor(c_u[:, 2 + a:2 + b], bank[c][:, 0:b - a], c_v[:, a:b], ALU.mult)
                            if c == NCH - 1:
                                ins = V.tensor_tensor(us[:, :, 2:], bank[c][:, b - a:CH].rearrange("p (b s) -> p b s", b=NB),
                                                      c_v[:, b:].rearrange("p (b s) -> p b s", b=NB), ALU.mult)
                            ins.then_inc(bank_free[c], 1)
                        dve.wait_ge(C_DVE.sem, C_DVE.at(j, "cw"))
                        for c in range(NCH):
                            dve.wait_ge(bank_free[c], emptied(4 * j + 2))
                        V.tensor_scalar(c_acc[:, 0:NP], c_u[:, 0:NP], c_w[:, 0:1], None, ALU.mult)
                        V.tensor_scalar(accs, us[:, :, 0:NS], c_w[:, 0:1], None, ALU.mult).then_inc(C_DVE.now("a0"), 1)
                        for w in (1, 2):
                            dve.wait_ge(C_DVE.sem, C_DVE.at(j, f"a{w - 1}"))
                            V.scalar_tensor_tensor(c_acc[:, 0:NP], c_u[:, w:w + NP], c_w[:, w:w + 1], c_acc[:, 0:NP],
                                                   ALU.mult, ALU.add)
                            V.scalar_tensor_tensor(accs, us[:, :, w:w + NS], c_w[:, w:w + 1], accs, ALU.mult,
                                                   ALU.add).then_inc(C_DVE.now(f"a{w}"), 1)
                        V.tensor_copy(c_last[:, bass.ds(j * 18, 2)], c_u[:, NP:NP + 2])
                        V.tensor_copy(c_last[:, bass.ds(j * 18 + 2, 16)].rearrange("p (b w) -> p b w", b=NB),
                                      us[:, :, NS:]).then_inc(C_DVE.now("last"), 1)
                    if t == 2:
                        dve.wait_ge(C_DVE.sem, C_DVE.at(j, "a2"))
                        for c in range(NCH):
                            dve.wait_ge(proj_done, n3 + (c + 1))
                            cols = slice(c * CH, (c + 1) * CH)
                            V.tensor_tensor(c_acc[:, cols], bank[c][:, 0:CH], c_acc[:, cols], ALU.mult).then_inc(bank_free[c], 1)
                    if t == 3:
                        for c in range(NCH):
                            dve.wait_ge(C_ACT.sem, C_ACT.at(j, f"g{c}"))
                            cols = slice(c * CH, (c + 1) * CH)
                            V.tensor_tensor(c_g[:, cols], bank[c][:, 0:CH], c_g[:, cols], ALU.mult).then_inc(bank_free[c], 1)
                            dve.wait_ge(bank_free[c], emptied(4 * j + 4))
                            V.tensor_tensor(c_o[:, cols], c_acc[:, cols], c_g[:, cols], ALU.mult).then_inc(C_DVE.now(f"o{c}"), 1)
                        for c in range(NCH):
                            dve.wait_ge(C_ACT.sem, C_ACT.at(j, f"h{c}"))
                            V.tensor_tensor(reg_b[:, bass.ds(KT * T + c * CH + j * T, CH)], c_o[:, c * CH:(c + 1) * CH],
                                            reg_b[:, bass.ds(j * T + c * CH, CH)].bitcast(F32),
                                            ALU.subtract).then_inc(C_DVE.now(f"l{c}"), 1)

            def col(n, what, r):
                at = 8 * (n % 2) + ("a", "b", "ms", "sd", "rs", "ms2", "sd2", "rs2").index(what)
                return small[0:r, at:at + 1]

            def scaled_y(n, r, V_ev, A_ev, sources, x_ready):
                dve.wait_ge(A_ev.sem, A_ev.at(n, "s1"))
                V.tensor_tensor(col(n, "ms", r), col(n, "a", r), col(n, "b", r), ALU.add).then_inc(V_ev.now("ms"), 1)
                dve.wait_ge(A_ev.sem, A_ev.at(n, "sd1"))
                V.reciprocal(col(n, "rs", r), col(n, "sd", r)).then_inc(V_ev.now("rs"), 1)
                dve.wait_ge(V_ev.sem, V_ev.at(n, "rs"))
                for half in range(2):
                    part = slice(half * HALF, (half + 1) * HALF)
                    V.scalar_tensor_tensor(o_t[0:r, part], sources[half][0:r, :], col(n, "rs", r), o_g[0:r, part],
                                           ALU.mult, ALU.mult).then_inc(V_ev.now(f"t{half}"), 1)
                dve.wait_ge(V_ev.sem, V_ev.at(n, "t1"))
                dve.wait_ge(xr_in[n % 3], x_ready)
                return V.tensor_tensor(o_x[n % 3][0:r, :], o_x[n % 3][0:r, :], o_t[0:r, :], ALU.add)

            def turned(i):
                r = rows_of(i)
                dst = o_tr[i % 2].rearrange("p (k t) -> p k t", k=KT)
                if i >= 2:
                    dve.wait_ge(A_TR.sem, A_TR.at(i - 2, "hi"))
                    dve.wait_ge(V_TR.sem, V_TR.at(i - 2, "lo"))
                for half, (name, g_name) in enumerate((("ta", "ga"), ("tb", "gb"))):
                    dve.wait_ge(P_TR.sem, P_TR.at(i, name))
                    src = bank[6 + half][:, :].rearrange("p (k t) -> p k t", k=4)[:, :, 0:r]
                    first = PRE + KT + 4 * half
                    g = cst[:, first:first + 4].unsqueeze(2).broadcast_to([P, 4, r])
                    V.tensor_tensor(dst[:, 4 * half:4 * half + 4, 0:r], src, g, ALU.mult).then_inc(V_TR.now(g_name), 1)

            def turned_lo(i):
                r = rows_of(i)
                hh, hl = halves(reg_b)
                dve.wait_ge(A_TR.sem, A_TR.at(i, "hi"))
                V.tensor_tensor(hl[:, :, i * P:i * P + r], o_tr[i % 2].rearrange("p (k t) -> p k t", k=KT)[:, :, 0:r],
                                hh[:, :, i * P:i * P + r].bitcast(F32), ALU.subtract).then_inc(V_TR.now("lo"), 1)

            for k in range(1, KT):
                hi, lo = [w.rearrange("p (k c) -> p k c", k=KT) for w in wout_tile(reg_a, k)]
                split_lo(NW1 + k + 1, k % 2, lo, hi)
            dve.wait_ge(g_in, 16)
            for i in range(TT):
                r = rows_of(i)
                if i:
                    dve.wait_ge(V_PO.sem, V_PO.at(i - 1, "x1"))
                scaled_y(i, r, V_PO, A_PO, [bank[2 * (i % 3) + half] for half in range(2)],
                         16 * (i // 3 + 1)).then_inc(V_PO.now("x1"), 1)
                if i:
                    turned(i - 1)
                dve.wait_ge(A_PO.sem, A_PO.at(i, "sd2"))
                V.reciprocal(col(i, "rs2", r), col(i, "sd2", r)).then_inc(V_PO.now("rs2"), 1)
                dve.wait_ge(V_PO.sem, V_PO.at(i, "rs2"))
                V.tensor_scalar(o_n[i % 2][0:r, :], o_x[i % 3][0:r, :], col(i, "rs2", r), None,
                                ALU.mult).then_inc(V_PO.now("xn"), 1)
                if i:
                    turned_lo(i - 1)
                if i == TT - 2:
                    split_lo(NW2 + 1, 0)
                    split_lo(NW2 + 2, 1)
            turned(TT - 1)
            turned_lo(TT - 1)

            def pairs(ap, m):
                v = ap.rearrange("p (b two r) -> p b two r", two=2, r=m)
                return v[:, :, 0, :], v[:, :, 1, :]

            def level(h, m):
                dve.wait_ge(VR.sem, VR.at(h, f"u{m // 2}"))
                dve.wait_ge(PR.sem, PR.at(h, f"L{m}"))
                nb = NP // (2 * m)
                kl, _ = pairs(r_K[:, 0:NP], m)
                _, qr = pairs(r_Q[:, 0:NP], m)
                tt = r_tt[:, 0:NP // 2].rearrange("p (b two r) -> p b two r", two=2, r=m // 2)[:, :, :, 0]
                tl, tr = tt[:, :, 0], tt[:, :, 1]
                V.tensor_tensor(qr, qr, tl.unsqueeze(2).broadcast_to([P, nb, m]), ALU.mult)
                V.tensor_tensor(kl, kl, tr.unsqueeze(2).broadcast_to([P, nb, m]), ALU.mult).then_inc(VR.now(f"w{m}"), 1)
                b = bank[3 + LEVELS.index(m) % 2]
                if m == 64:
                    dst = r_am[0:64, :].rearrange("p (c t) -> p c t", c=CK)[:, :, 64:]
                    ins = V.tensor_copy(dst, b[0:64, :].rearrange("p (c t) -> p c t", c=CK))
                else:
                    dst = r_am.rearrange("p (c b two r) -> p c b two r", c=CK, two=2, r=m)[:, :, :, 1, :]
                    shape = [P, CK, 64 // m, m]
                    mask = masks[m][:, :].rearrange("p (b r) -> p b r", r=m)
                    ins = V.copy_predicated(dst, mask.unsqueeze(1).broadcast_to(shape),
                                            b[:, :].rearrange("p (c b r) -> p c b r", c=CK, r=m))
                ins.then_inc(VR.now(f"c{m}"), 1)
                dve.wait_ge(VR.sem, VR.at(h, f"w{m}"))
                V.tensor_tensor(tl, tl, tr, ALU.mult).then_inc(VR.now(f"u{m}"), 1)

            def every(ap, n, i):
                return ap.rearrange("p (b n) -> p b n", n=n)[:, :, i]

            def prepare(h):
                V.tensor_copy(lbh[:, :].unsqueeze(2), lb[:, :, bass.ds(h, 1)]).then_inc(VR.now("lb"), 1)
                for c in range(NCH):
                    dve.wait_ge(bank_free[c], emptied(bank_use(NW2) + 3 + 4 * h))
                V.tensor_copy(r_Q, r_q).then_inc(VR.now("qc"), 1)
                dve.wait_ge(VR.sem, VR.at(h, "lb"))
                V.tensor_scalar(r_K, r_kr, lbh[:, 1:2], None, ALU.mult).then_inc(VR.now("k"), 1)
                V.tensor_scalar(r_f, r_f, lbh[:, 1:2], lbh[:, 0:1], ALU.mult, ALU.add).then_inc(VR.now("fa"), 1)
                dve.wait_ge(VR.sem, VR.at(h, "fa"))
                V.tensor_scalar(r_f, r_f, F_FLOOR, None, ALU.max).then_inc(VR.now("f"), 1)
                dve.wait_ge(VR.sem, VR.at(h, "f"))
                V.tensor_tensor(r_tt[:, :], every(r_f, 2, 0), every(r_f, 2, 1), ALU.mult).then_inc(VR.now("tt"), 1)

            def gate(h):
                dve.wait_ge(ot_done, h + 1)
                for a, b, src in ((0, 512, bank[5][:, :]), (512, NP, bank[6][:, :]), (NP, T, bank[7][:, 256:256 + NSAMP])):
                    ins = V.scalar_tensor_tensor(r_o[:, a:b], src, cst[:, ONRM:ONRM + 1], r_g[:, a:b], ALU.mult, ALU.mult)
                ins.then_inc(o_rdy, 1)

            def turn_lo(h):
                dve.wait_ge(o_hi, h + 1)
                V.tensor_tensor(reg_a[:, bass.ds(h * T + KT * T, T)], r_o, reg_a[:, bass.ds(h * T, T)].bitcast(F32),
                                ALU.subtract).then_inc(o_lo, 1)

            def rec(h, s, last):
                inv_f = r_am[:, 0:T // 2].rearrange("p (b two) -> p b two", two=2)
                inv_t = r_am[:, T // 2:3 * T // 4]
                if s == 0:
                    if last is not None:
                        gate(last)
                    dve.wait_ge(VR.sem, VR.at(h, "tt"))
                    V.reciprocal(inv_f, r_f.rearrange("p (b n) -> p b n", n=B4)[:, :, 1:3]).then_inc(VR.now("rf"), 1)
                    V.reciprocal(inv_t, every(r_tt[:, :], 2, 1)).then_inc(VR.now("rt"), 1)
                elif s == 1:
                    dve.wait_ge(VR.sem, VR.at(h, "rt"))
                    for ap, i, factor, name in ((r_Q, 0, inv_f[:, :, 0], "q0"), (r_Q, 2, every(r_f, B4, 2), "q2"),
                                                (r_Q, 3, every(r_tt[:, :], 2, 1), "q3"),
                                                (r_K, 0, every(r_f, B4, 1), "k0"), (r_K, 2, inv_f[:, :, 1], "k2"),
                                                (r_K, 3, inv_t, "k3")):
                        V.tensor_tensor(every(ap, B4, i), every(ap, B4, i), factor, ALU.mult).then_inc(VR.now(name), 1)
                    dve.wait_ge(PR.sem, PR.at(h, "vt"))
                    V.tensor_copy(r_vt[0:NSAMP, CK * P:], bank[7][0:NSAMP, P:2 * P]).then_inc(VR.now("vs"), 1)
                    if last is not None:
                        turn_lo(last)
                elif s == 3:
                    dve.wait_ge(PR.sem, PR.at(h, "dg"))
                    dve.wait_ge(VR.sem, VR.at(h, "k3"))
                    for half in range(2):
                        ins = V.tensor_tensor(r_am[:, half * 512:(half + 1) * 512].rearrange("p (c t) -> p c t", c=4),
                                              bank[3 + half][:, :].rearrange("p (c t) -> p c t", c=4),
                                              mask4[:, :].unsqueeze(1).broadcast_to([P, 4, P]), ALU.mult)
                    ins.then_inc(VR.now("am"), 1)
                    V.tensor_tensor(r_as[:, :], bank[7][0:NSAMP, 0:NSAMP], mask4[0:NSAMP, 0:NSAMP],
                                    ALU.mult).then_inc(VR.now("as"), 1)
                    four = [ap.rearrange("p (b n) -> p b n", n=B4) for ap in (r_Q, r_K)]
                    for i, ap in enumerate(four):
                        ins = V.tensor_tensor(ap, ap, every(r_tt[:, :], 2, i).unsqueeze(2).broadcast_to([P, T // B4, B4]),
                                              ALU.mult)
                    ins.then_inc(VR.now("w2"), 1)
                    dve.wait_ge(VR.sem, VR.at(h, "w2"))
                    V.tensor_tensor(every(r_tt[:, :], 2, 0), every(r_tt[:, :], 2, 0), every(r_tt[:, :], 2, 1),
                                    ALU.mult).then_inc(VR.now("u2"), 1)
                    V.tensor_copy(r_qb[:, :].rearrange("p (b s) -> p b s", b=NB)[:, :, 0:NS],
                                  r_Q[:, NP:].rearrange("p (b s) -> p b s", b=NB)).then_inc(VR.now("qb"), 1)
                elif 4 <= s <= 6:
                    level(h, 1 << (s - 2))
                elif s == 7:
                    level(h, 32)
                    dve.wait_ge(PR.sem, PR.at(h, "us"))
                    dve.wait_ge(VR.sem, VR.at(h, "u2"))
                    st = r_s.rearrange("p (b v) -> p b v", b=NB)
                    tot = r_tt[:, NP // 2:].rearrange("p (b two) -> p b two", two=2)[:, :, 0]
                    V.tensor_tensor(st, st, tot.unsqueeze(2).broadcast_to([P, NB, P]), ALU.mult).then_inc(VR.now("ss"), 1)
                    dve.wait_ge(VR.sem, VR.at(h, "ss"))
                    for half, name in enumerate(("sn0", "snew")):
                        V.tensor_tensor(r_s[:, half * 512:(half + 1) * 512], r_s[:, half * 512:(half + 1) * 512],
                                        bank[5 + half][:, :], ALU.add).then_inc(VR.now(name), 1)
                    level(h, 64)
                elif s == 9:
                    dve.wait_ge(PR.sem, PR.at(h, "u"))
                    dve.wait_ge(s0_out, h * 16 + 16)
                    for c in range(CK):
                        cols = slice(c * P, (c + 1) * P)
                        src = bank[5 + c // 4][:, (c % 4) * P:(c % 4 + 1) * P]
                        if c == 0:
                            ins = V.tensor_copy(r_s[:, cols], src)
                        else:
                            dve.wait_ge(VR.sem, VR.at(h, f"s{c - 1}"))
                            ins = V.scalar_tensor_tensor(r_s[:, cols], r_s[:, (c - 1) * P:c * P], r_tt[:, c * 64:c * 64 + 1],
                                                         src, ALU.mult, ALU.add)
                        ins.then_inc(VR.now(f"s{c}"), 1)
                elif s == 10:
                    for half in range(2):
                        dve.wait_ge(AR.sem, AR.at(h, f"sq{half}"))
                        V.tensor_reduce(small[:, 4 * half:4 * half + 4], r_sq[:, half * 512:(half + 1) * 512]
                                        .rearrange("p (c v) -> p c v", c=4), AX.X, ALU.add).then_inc(VR.now(f"r{half}"), 1)
                    dve.wait_ge(AR.sem, AR.at(h, "sd"))
                    V.reciprocal(small[:, 32:32 + CK], small[:, 16:16 + CK]).then_inc(VR.now("rs"), 1)
                    dve.wait_ge(AR.sem, AR.at(h, "sds"))
                    V.reciprocal(small[0:NSAMP, 32 + CK:33 + CK], small[0:NSAMP, 16 + CK:17 + CK]).then_inc(VR.now("rss"), 1)
                    dve.wait_ge(VR.sem, VR.at(h, "rss"))
                    for half in range(2):
                        V.tensor_tensor(r_kt[:, half * 512:(half + 1) * 512].rearrange("p (c v) -> p c v", c=4),
                                        bank[3 + half][:, :].rearrange("p (c v) -> p c v", c=4),
                                        small[:, 32 + 4 * half:36 + 4 * half].unsqueeze(2).broadcast_to([P, 4, P]),
                                        ALU.mult).then_inc(VR.now(f"on{half}"), 1)
                    V.tensor_scalar(r_kt[0:NSAMP, CK * P:], r_os[0:NSAMP, :], small[0:NSAMP, 32 + CK:33 + CK], None,
                                    ALU.mult).then_inc(VR.now("ons"), 1)

            def evac(kind, c, j):
                sig, buf = (q_sig, r_q) if kind == "q" else (z_sig, r_g)
                cols = slice(c * CH, (c + 1) * CH)
                dve.wait_ge(sig, 3 * j + (c + 1))
                V.scalar_tensor_tensor(buf[:, cols], buf[:, cols], QSCALE if kind == "q" else 1.0, bank[c][:, 0:CH],
                                       ALU.mult, ALU.mult).then_inc(bank_free[c], 1)

            for c in range(NCH):
                evac("q", c, 0)
            split_lo(NW2 + 3, 0)
            split_lo(NW2 + 4, 1)
            for k in range(3):
                dve.wait_ge(stored[k], 48)

            def iteration(j, last):
                prepare(j - 1)
                for t, kind in enumerate("qzvf"):
                    for c in range(NCH):
                        if kind == "q":
                            evac("q", c, j)
                        elif kind == "z":
                            evac("z", c, j - 1)
                        rec(j - 1, 3 * t + c, last)
                        if c == 0:
                            split_lo(4 * j + (NW2 + t + 1), t % 2)

            iteration(1, None)
            with dve.Fori(2, KT) as j:
                iteration(j, j - 2)
            prepare(KT - 1)
            split_lo(NW3 + 1, 0)
            for s in range(12):
                if 2 <= s < 5:
                    evac("z", s - 2, KT - 1)
                rec(KT - 1, s, KT - 2)
                for k in SPLIT_OUT.get(s, ()):
                    hi, lo = [w.rearrange("p (k c) -> p k c", k=KT) for w in wout_tile(reg_b, k)]
                    split_lo(NW3 + k + 1, k % 2, lo, hi)
            gate(KT - 1)
            turn_lo(KT - 1)

            dve.wait_ge(g_in, 32)
            for n, i in enumerate(ORDER2):
                r = rows_of(i)
                if n:
                    dve.wait_ge(V_P2.sem, V_P2.at(n - 1, "x"))
                sources = [bank[2 * (n % 4) + half] for half in range(2)]
                if i < PARTS:
                    dve.wait_ge(y_done, TT + n + 1)
                    dve.wait_ge(part_moved, 2 * i + 2)
                    for half in range(2):
                        V.tensor_tensor(o_part(i, half), o_part(i, half), sources[half][:, :],
                                        ALU.add).then_inc(V_Y.now(f"y{half}"), 1)
                    sources = [o_part(i, half) for half in range(2)]
                scaled_y(n, r, V_P2, A_P2, sources, 48 + 16 * (n // 3 + 1)).then_inc(V_P2.now("x"), 1)


_INS = ["x_prompt", "x_sample", "state_conv", "state_hgrn", "norm_pre", "w_in", "conv_w", "hgrn_lb_logits",
        "hgrn_onorm", "w_out", "norm_post"]
_OUTS = [(1, NP, D), (NB, NS, D), (1, 1, 2, D), (1, NB, 2, D), (1, 1, KT, P, P), (1, NB, KT, P, P)]


def kernel(**inputs):
    import numpy as _np
    import concourse.bacc as _bacc
    from concourse.bass_utils import run_bass_kernel_spmd as _run

    nc = _bacc.Bacc("TRN2", target_bir_lowering=False, num_devices=1)
    arrays, args = {}, []
    for name in _INS:
        a = _np.ascontiguousarray(inputs[name])
        arrays[f"in_{name}"] = a
        args.append(nc.dram_tensor(f"in_{name}", a.shape, F32, kind="ExternalInput").ap())
    for i, shape in enumerate(_OUTS):
        args.append(nc.dram_tensor(f"out_{i}", shape, F32, kind="ExternalOutput").ap())
    build(nc, *args)
    r = _run(nc, [arrays], core_ids=[0])
    return tuple(r.results[0][f"out_{i}"] for i in range(len(_OUTS)))
```
